# Optimizing a Trainium2 kernel written in Bass

```python
import math
import jax, jax.numpy as jnp
from jax import lax
import numpy as np

D_MODEL = 1024
BATCH = 1
SEQ = 256
DEPTH = 2

N_MIXERS = 3
BLOCK = 128
RMS_EPS = 1e-6

SWA_HEADS = 16
SWA_KV_HEADS = 2
SWA_HEAD_DIM = 64
SWA_WINDOW = 128

REL_BUCKETS = 32
REL_MAX_DIST = 128

SB_HEADS = 16
SB_HEAD_DIM = 64

MLA_HEADS = 16
MLA_NOPE_DIM = 64
MLA_ROPE_DIM = 32
MLA_V_DIM = 64
MLA_Q_RANK = 384
MLA_KV_RANK = 256
ROPE_THETA = 10000.0

FFN_DIM = 2816
N_EXPERTS = 8
TOP_K = 2
EXPERT_DIM = 3584

kernel_name = 'hybrid_swa_stickbreak_mla_moe_trunk'

def rms_norm(x, g):
    xf = x.astype(jnp.float32)
    y = xf * lax.rsqrt(jnp.mean(xf * xf, axis=-1, keepdims=True) + RMS_EPS)
    return (y * g.astype(jnp.float32)).astype(x.dtype)

def t5_causal_bucket(dist):
    max_exact = REL_BUCKETS // 2
    d = jnp.maximum(dist, 1).astype(jnp.float32)
    large = max_exact + (jnp.log(d / max_exact) / math.log(REL_MAX_DIST / max_exact)
                         * (REL_BUCKETS - max_exact)).astype(jnp.int32)
    large = jnp.minimum(large, REL_BUCKETS - 1)
    return jnp.where(dist < max_exact, dist, large)

def rope_tables(seq, dim):
    inv = ROPE_THETA ** (-jnp.arange(0, dim, 2, dtype=jnp.float32) / dim)
    ang = jnp.arange(seq, dtype=jnp.float32)[:, None] * inv[None, :]
    return jnp.cos(ang), jnp.sin(ang)

def apply_rope(x, cos, sin):
    x1, x2 = jnp.split(x, 2, axis=-1)
    c = cos[None, :, None, :].astype(x.dtype)
    s = sin[None, :, None, :].astype(x.dtype)
    return jnp.concatenate([x1 * c - x2 * s, x1 * s + x2 * c], axis=-1)

def swa_sink_attention(h, w_qkv, b_qkv, sinks, w_o, rel_bias):
    B, S, _ = h.shape
    nb = S // BLOCK
    G = SWA_HEADS // SWA_KV_HEADS
    qkv = h @ w_qkv + b_qkv
    q, k, v = jnp.split(qkv, [SWA_HEADS * SWA_HEAD_DIM,
                              (SWA_HEADS + SWA_KV_HEADS) * SWA_HEAD_DIM], axis=-1)
    q = q.reshape(B, nb, BLOCK, SWA_KV_HEADS, G, SWA_HEAD_DIM)
    k = k.reshape(B, nb, BLOCK, SWA_KV_HEADS, SWA_HEAD_DIM)
    v = v.reshape(B, nb, BLOCK, SWA_KV_HEADS, SWA_HEAD_DIM)

    def with_prev(t):
        prev = jnp.pad(t[:, :-1], ((0, 0), (1, 0), (0, 0), (0, 0), (0, 0)))
        return jnp.concatenate([prev, t], axis=2)

    kb, vb = with_prev(k), with_prev(v)
    s = jnp.einsum('bnqhgd,bnkhd->bnhgqk', q, kb).astype(jnp.float32) * (SWA_HEAD_DIM ** -0.5)

    qi = jnp.arange(BLOCK)[:, None]
    kj = jnp.arange(2 * BLOCK)[None, :]
    dist = qi + BLOCK - kj
    bias = rel_bias.astype(jnp.float32)[t5_causal_bucket(jnp.maximum(dist, 0))]
    bias = bias.transpose(2, 0, 1).reshape(SWA_KV_HEADS, G, BLOCK, 2 * BLOCK)
    band = (dist >= 0) & (dist < SWA_WINDOW)
    valid = band[None] & ((jnp.arange(nb)[:, None, None] > 0) | (kj[None] >= BLOCK))
    s = jnp.where(valid[None, :, None, None], s + bias, -jnp.inf)

    sink = jnp.broadcast_to(sinks.astype(jnp.float32).reshape(1, 1, SWA_KV_HEADS, G, 1, 1),
                            s.shape[:-1] + (1,))
    p = jax.nn.softmax(jnp.concatenate([s, sink], axis=-1), axis=-1)[..., :-1]
    o = jnp.einsum('bnhgqk,bnkhd->bnqhgd', p.astype(vb.dtype), vb)
    return o.reshape(B, S, SWA_HEADS * SWA_HEAD_DIM) @ w_o

def stick_breaking_attention(h, w_qkv, w_o):
    B, S, _ = h.shape
    nb = S // BLOCK
    q, k, v = jnp.split(h @ w_qkv, 3, axis=-1)
    q = q.reshape(B, nb, BLOCK, SB_HEADS, SB_HEAD_DIM).transpose(1, 0, 3, 2, 4)
    k = k.reshape(B, S, SB_HEADS, SB_HEAD_DIM)
    v = v.reshape(B, S, SB_HEADS, SB_HEAD_DIM)
    key_pos = jnp.arange(S)
    scale = SB_HEAD_DIM ** -0.5

    def block(args):
        qb, b_idx = args
        z = jnp.einsum('bhqd,bkhd->bhqk', qb, k).astype(jnp.float32) * scale
        q_pos = b_idx * BLOCK + jnp.arange(BLOCK)
        before = key_pos[None, :] < q_pos[:, None]
        log_fail = jnp.where(before, jax.nn.log_sigmoid(-z), 0.0)
        between = lax.cumsum(log_fail, axis=3, reverse=True) - log_fail
        a = jnp.where(before, jnp.exp(jax.nn.log_sigmoid(z) + between), 0.0)
        return jnp.einsum('bhqk,bkhd->bqhd', a.astype(v.dtype), v)

    o = lax.map(block, (q, jnp.arange(nb)))
    o = o.transpose(1, 0, 2, 3, 4).reshape(B, S, SB_HEADS * SB_HEAD_DIM)
    return o @ w_o

def causal_attention_blocked(q, k, v, scale):
    B, S, H, _ = q.shape
    nb = S // BLOCK
    qb = q.reshape(B, nb, BLOCK, H, -1).transpose(1, 0, 2, 3, 4)
    key_pos = jnp.arange(S)

    def block(args):
        qblk, b_idx = args
        s = jnp.einsum('bqhd,bkhd->bhqk', qblk, k).astype(jnp.float32) * scale
        q_pos = b_idx * BLOCK + jnp.arange(BLOCK)
        s = jnp.where(key_pos[None, :] <= q_pos[:, None], s, -jnp.inf)
        p = jax.nn.softmax(s, axis=-1).astype(v.dtype)
        return jnp.einsum('bhqk,bkhd->bqhd', p, v)

    o = lax.map(block, (qb, jnp.arange(nb)))
    return o.transpose(1, 0, 2, 3, 4).reshape(B, S, H * v.shape[-1])

def mla_attention(h, w_down, q_norm, w_uq, kv_norm, w_ukv, w_o):
    B, S, _ = h.shape
    c = h @ w_down
    c_q, c_kv, k_rope = jnp.split(c, [MLA_Q_RANK, MLA_Q_RANK + MLA_KV_RANK], axis=-1)
    cos, sin = rope_tables(S, MLA_ROPE_DIM)
    q = (rms_norm(c_q, q_norm) @ w_uq).reshape(B, S, MLA_HEADS, MLA_NOPE_DIM + MLA_ROPE_DIM)
    q_nope, q_rope = jnp.split(q, [MLA_NOPE_DIM], axis=-1)
    q_rope = apply_rope(q_rope, cos, sin)
    kv = (rms_norm(c_kv, kv_norm) @ w_ukv).reshape(B, S, MLA_HEADS, MLA_NOPE_DIM + MLA_V_DIM)
    k_nope, v = jnp.split(kv, [MLA_NOPE_DIM], axis=-1)
    k_rope = apply_rope(k_rope[:, :, None, :], cos, sin)
    q_cat = jnp.concatenate([q_nope, q_rope], axis=-1)
    k_cat = jnp.concatenate([k_nope, jnp.broadcast_to(k_rope, (B, S, MLA_HEADS, MLA_ROPE_DIM))], axis=-1)
    o = causal_attention_blocked(q_cat, k_cat, v, (MLA_NOPE_DIM + MLA_ROPE_DIM) ** -0.5)
    return o @ w_o

def swiglu(h, w_gate, w_up, w_down):
    return (jax.nn.silu(h @ w_gate) * (h @ w_up)) @ w_down

def moe_swiglu(h, router, w_gate, w_up, w_down):
    B, S, D = h.shape
    t = h.reshape(B * S, D)
    logits = (t @ router).astype(jnp.float32)
    top_vals, top_idx = lax.top_k(logits, TOP_K)
    gates = jax.nn.softmax(top_vals, axis=-1)
    combine = jnp.sum(jax.nn.one_hot(top_idx, N_EXPERTS, dtype=jnp.float32) * gates[..., None], axis=1)
    out = jnp.zeros_like(t)
    for e in range(N_EXPERTS):
        out = out + combine[:, e:e + 1].astype(t.dtype) * swiglu(t, w_gate[e], w_up[e], w_down[e])
    return out.reshape(B, S, D)

def _n_layers_of(mixer_id):
    return len(range(mixer_id, DEPTH, N_MIXERS))

def setup_inputs(seed: int = 0) -> dict:
    key = jax.random.key(seed)
    ks = jax.random.split(key, 24)
    f32 = jnp.float32
    nA, nB, nC = _n_layers_of(0), _n_layers_of(1), _n_layers_of(2)
    n_dense, n_moe = len(range(0, DEPTH, 2)), len(range(1, DEPTH, 2))

    def w(k, shape, fan_in):
        return jax.random.normal(k, shape, f32) * (fan_in ** -0.5)

    def gain(k, shape):
        return 1.0 + 0.02 * jax.random.normal(k, shape, f32)

    qkv_a = (SWA_HEADS + 2 * SWA_KV_HEADS) * SWA_HEAD_DIM
    mla_down = MLA_Q_RANK + MLA_KV_RANK + MLA_ROPE_DIM
    return {
        'x': jax.random.normal(ks[0], (BATCH, SEQ, D_MODEL), f32),
        'rel_bias': 0.5 * jax.random.normal(ks[1], (REL_BUCKETS, SWA_HEADS), f32),
        'attn_norm': gain(ks[2], (DEPTH, D_MODEL)),
        'ffn_norm': gain(ks[3], (DEPTH, D_MODEL)),
        'final_norm': gain(ks[4], (D_MODEL,)),
        'swa_w_qkv': w(ks[5], (nA, D_MODEL, qkv_a), D_MODEL),
        'swa_b_qkv': 0.02 * jax.random.normal(ks[6], (nA, qkv_a), f32),
        'swa_sinks': 0.5 * jax.random.normal(ks[7], (nA, SWA_HEADS), f32),
        'swa_w_o': w(ks[8], (nA, SWA_HEADS * SWA_HEAD_DIM, D_MODEL), SWA_HEADS * SWA_HEAD_DIM),
        'sb_w_qkv': w(ks[9], (nB, D_MODEL, 3 * SB_HEADS * SB_HEAD_DIM), D_MODEL),
        'sb_w_o': w(ks[10], (nB, SB_HEADS * SB_HEAD_DIM, D_MODEL), SB_HEADS * SB_HEAD_DIM),
        'mla_w_down': w(ks[11], (nC, D_MODEL, mla_down), D_MODEL),
        'mla_q_norm': gain(ks[12], (nC, MLA_Q_RANK)),
        'mla_w_uq': w(ks[13], (nC, MLA_Q_RANK, MLA_HEADS * (MLA_NOPE_DIM + MLA_ROPE_DIM)), MLA_Q_RANK),
        'mla_kv_norm': gain(ks[14], (nC, MLA_KV_RANK)),
        'mla_w_ukv': w(ks[15], (nC, MLA_KV_RANK, MLA_HEADS * (MLA_NOPE_DIM + MLA_V_DIM)), MLA_KV_RANK),
        'mla_w_o': w(ks[16], (nC, MLA_HEADS * MLA_V_DIM, D_MODEL), MLA_HEADS * MLA_V_DIM),
        'ffn_w_gate': w(ks[17], (n_dense, D_MODEL, FFN_DIM), D_MODEL),
        'ffn_w_up': w(ks[18], (n_dense, D_MODEL, FFN_DIM), D_MODEL),
        'ffn_w_down': w(ks[19], (n_dense, FFN_DIM, D_MODEL), FFN_DIM),
        'moe_router': w(ks[20], (n_moe, D_MODEL, N_EXPERTS), D_MODEL),
        'moe_w_gate': w(ks[21], (n_moe, N_EXPERTS, D_MODEL, EXPERT_DIM), D_MODEL),
        'moe_w_up': w(ks[22], (n_moe, N_EXPERTS, D_MODEL, EXPERT_DIM), D_MODEL),
        'moe_w_down': w(ks[23], (n_moe, N_EXPERTS, EXPERT_DIM, D_MODEL), EXPERT_DIM),
    }

def reference(x, rel_bias, attn_norm, ffn_norm, final_norm,
              swa_w_qkv, swa_b_qkv, swa_sinks, swa_w_o,
              sb_w_qkv, sb_w_o,
              mla_w_down, mla_q_norm, mla_w_uq, mla_kv_norm, mla_w_ukv, mla_w_o,
              ffn_w_gate, ffn_w_up, ffn_w_down,
              moe_router, moe_w_gate, moe_w_up, moe_w_down):
    for i in range(DEPTH):
        h = rms_norm(x, attn_norm[i])
        mixer, j = i % N_MIXERS, i // N_MIXERS
        if mixer == 0:
            mix = swa_sink_attention(h, swa_w_qkv[j], swa_b_qkv[j], swa_sinks[j], swa_w_o[j], rel_bias)
        elif mixer == 1:
            mix = stick_breaking_attention(h, sb_w_qkv[j], sb_w_o[j])
        else:
            mix = mla_attention(h, mla_w_down[j], mla_q_norm[j], mla_w_uq[j],
                                mla_kv_norm[j], mla_w_ukv[j], mla_w_o[j])
        x = x + mix
        h = rms_norm(x, ffn_norm[i])
        f = i // 2
        if i % 2 == 0:
            x = x + swiglu(h, ffn_w_gate[f], ffn_w_up[f], ffn_w_down[f])
        else:
            x = x + moe_swiglu(h, moe_router[f], moe_w_gate[f], moe_w_up[f], moe_w_down[f])
    return rms_norm(x, final_norm)


_drawn_inputs = setup_inputs


def setup_inputs(seed=0):
    import zlib

    import numpy as np

    out = dict(_drawn_inputs(seed))
    spreads = {}
    factors = {'final_norm': 2.872, 'swa_sinks': 5.349}
    for name, (base, spread) in spreads.items():
        noise = np.random.default_rng([zlib.crc32(name.encode()), seed]).standard_normal(out[name].shape)
        drawn = base * np.exp(spread * noise) if base else spread * noise
        out[name] = __import__('jax').numpy.asarray(drawn.astype(out[name].dtype))
    for name, factor in factors.items():
        out[name] = (out[name] * factor).astype(out[name].dtype)
    return out
```

```python
from contextlib import ExitStack

import numpy as np
import concourse.bass as bass
from concourse import mybir

F32 = mybir.dt.float32
I32 = mybir.dt.int32
ALU = mybir.AluOpType
ACT = mybir.ActivationFunctionType
AX = mybir.AxisListType

P = 128
SEQ, D = 256, 1024
TB = SEQ // P
DT = D // P
HALF = 512
DH = D // HALF
H, HD = 16, 64
FT = H * HD // P
KV = 2
WINDOW = 128
GROUP = 4
BUCKETS, MAX_DIST = 32, 128
FFN = 2816
FFN_TILES = FFN // P
UNITS = FFN_TILES // 2
E, EDIM = 8, 3584
BLOCKS = EDIM // HALF
BT = HALF // P
CAP = 96
PASSES = -(-SEQ // CAP)
EPS = 1e-6
SCALE = HD ** -0.5
MASKED = -1e30
SOFT_TOP = 30.0

RING = 7
Q_LOADS = 3
N_WO0 = Q_LOADS
N_FFN = N_WO0 + DH
FFN_BLOCKS = -(-FFN_TILES // BT)
N_QKV1 = N_FFN + 3 * FFN_BLOCKS
N_WO1 = N_QKV1 + 6
N_MOE = N_WO1 + DH
MOE_LOADS = 3 * BLOCKS
assert MOE_LOADS % RING == 0


def moe_order():
    order = []
    for b in range(BLOCKS):
        order += [("gate", b), ("up", b)] + ([("down", b - 1)] if b else [])
    return order + [("down", BLOCKS - 1)]


MOE_ORDER = moe_order()
MOE_AT = {key: k for k, key in enumerate(MOE_ORDER)}

C_IDENT, C_TRI, C_BEFORE, C_FLIP, C_IOTA = 0, P, 2 * P, 3 * P, 4 * P
C_DESC = C_IOTA + CAP
C_COLS = C_DESC + E


def constants():
    c = np.zeros((P, C_COLS), np.float32)
    i, j = np.arange(P)[:, None], np.arange(P)[None, :]
    c[:, C_IDENT:C_IDENT + P] = i == j
    c[:, C_TRI:C_TRI + P] = -(i >= j).astype(np.float32)
    c[:, C_BEFORE:C_BEFORE + P] = i < j
    c[:, C_FLIP:C_FLIP + P] = i + j == P - 1
    c[:, C_IOTA:C_IOTA + CAP] = np.arange(CAP)
    c[:, C_DESC:C_DESC + E] = E - np.arange(E)
    return c


def bucket_rows():
    dist = (-np.arange(2 * WINDOW)) % WINDOW
    exact = BUCKETS // 2
    far = np.maximum(dist, 1).astype(np.float32)
    large = exact + (np.log(far / np.float32(exact)) / np.float32(np.log(MAX_DIST / exact))
                     * np.float32(BUCKETS - exact)).astype(np.int32)
    bucket = np.where(dist < exact, dist, np.minimum(large, BUCKETS - 1))
    return (np.arange(BUCKETS)[:, None] == bucket[None, :]).astype(np.float32)


class Uses:

    def __init__(self):
        self.at, self.fills, self.frees, self.next = {}, [0] * 8, [0] * 8, 0

    def use(self, key, bank=None, counted=True):
        if bank is None:
            bank = self.next
            self.next = (bank + 1) % 8
        self.at[key] = (bank, self.fills[bank], self.frees[bank])
        self.fills[bank] += 1
        self.frees[bank] += counted


def plan():
    u = Uses()
    u.use("vectors")
    u.use("bias rows")

    def transposed(name):
        for j in range(4):
            u.use((name, j))

    transposed("hT0")
    for j in range(FT // 2):
        u.use(("q", j))
    u.use("k")
    u.use("v")
    for n in range(4):
        u.use(("toeplitz", n))
    for g in range(H // GROUP + 2):
        if g < H // GROUP:
            for half in range(2):
                u.use(("s1", g, half))
                u.use(("s0", g, half))
        if 1 <= g <= H // GROUP:
            for t in range(3):
                u.use(("pT", g - 1, t))
        if g >= 2:
            u.use(("o", g - 2))
    transposed("oT0")
    for dh in range(DH):
        for tb in range(TB):
            u.use(("wo0", dh, tb))
    transposed("hT1")
    for n in range(UNITS):
        u.use(("fg", n), n % 2)
        u.use(("fu", n), 2 + n % 2)
    for tb in range(TB):
        for dh in range(DH):
            u.use(("fy", tb, dh), 4 + 2 * tb + dh)
    transposed("hT2")
    for j in range(FT // 2):
        u.use(("q1", j))
    for j in range(FT // 2):
        u.use(("k1", j))
    for vh in range(2):
        for tb in range(TB):
            u.use(("v1", vh, tb))
    for b in range(FT):
        for half in range(2):
            u.use(("z", b, half), (2 * b + half) % 6)
    for n in range(FT // 2):
        u.use(("so", n), 6 + n % 2)
    transposed("oT1")
    for dh in range(DH):
        for tb in range(TB):
            u.use(("wo1", dh, tb))
    transposed("hT3")
    u.use("logits")
    u.use("places")
    u.use(("first gather", 0), 6, counted=False)
    u.use(("first gather", 1), 7, counted=False)
    fills, frees = list(u.fills), list(u.frees)
    for b in range(BLOCKS):
        u.use(("g", b), b % 2)
        u.use(("u", b), 2 + b % 2)
    for dh in range(DH):
        u.use(("y", dh), 4 + dh)
    u.use("gates", 6)
    u.use(("gather", 0), 6, counted=False)
    u.use(("gather", 1), 7, counted=False)
    for n in range(TB * DH):
        u.use(("scatter", n), 7 - n % 2)
    return u.at, [b - a for a, b in zip(fills, u.fills)], [b - a for a, b in zip(frees, u.frees)]


USES, FILLS, FREES = plan()
IN_LOOP = {"g", "u", "y", "gates", "gather", "scatter"}


def looped(key):
    return (key if isinstance(key, str) else key[0]) in IN_LOOP


class Steps:

    def __init__(self, engine, sem):
        self.engine, self.sem, self.n, self.i, self.each = engine, sem, 0, None, 0

    def mark(self, instruction):
        instruction.then_inc(self.sem, 1)
        self.n += 1

    def settle(self):
        self.engine.wait_ge(self.sem, self.n if self.i is None else self.i * self.each + self.n)

    def loop(self, i, each):
        self.i, self.each, self.start = i, each, self.n

    def end(self):
        assert self.n - self.start == self.each, (self.n - self.start, self.each)


def build(nc, a):
    ctx = ExitStack()
    with ctx:
        def sb(name, shape, dt=F32):
            return ctx.enter_context(nc.sbuf_tensor(name, shape, dt))

        def sem(name):
            return ctx.enter_context(nc.semaphore(name))

        ring = [sb(f"weights{n}", [P, DT, HALF]) for n in range(RING)]
        x = sb("x", [P, TB, D])
        h = sb("h", [P, TB, D])
        hT = sb("hT", [P, DT, SEQ])
        qT = sb("qT", [P, FT, SEQ])
        o = sb("o", [P, TB, D])
        oT = sb("oT", [P, DT, SEQ])
        kv_area = sb("kv_area", [P, 4096])
        work = sb("work", [P, 3072])
        consts = sb("consts", [P, C_COLS])
        ones = sb("ones", [P, P])
        minus_ones = sb("minus_ones", [P, P])
        vec_rows = sb("vec_rows", [42, P])
        vec = sb("vec", [P, 42])
        final_gain = sb("final_gain", [P, D])
        v_bias = sb("v_bias", [1, KV * HD])
        sinks = sb("sinks", [P, H])
        minus_sinks = sb("minus_sinks", [P, H])
        k_swa = sb("k_swa", [P, SEQ])
        kT_swa = sb("kT_swa", [P, KV, SEQ])
        v_swa = sb("v_swa", [P, TB, KV * HD])
        rel = sb("rel", [BUCKETS, H])
        onehot = sb("onehot", [BUCKETS, 2 * WINDOW])
        router = sb("router", [P, DT, E])
        sumsq = sb("sumsq", [P, TB])
        meansq = sb("meansq", [P, TB])
        root = sb("root", [P, TB])
        rstd = sb("rstd", [P, TB])
        peak = sb("peak", [P, 2, TB, GROUP])
        shift = sb("shift", [P, 2, TB, GROUP])
        sink_gap = sb("sink_gap", [P, 2, TB, GROUP])
        sink_exp = sb("sink_exp", [P, 2, TB, GROUP])
        row_sum = sb("row_sum", [P, 2, TB, GROUP])
        total = sb("total", [P, 2, TB, GROUP])
        inverse = sb("inverse", [P, 2, TB, GROUP])
        route = sb("route", [P, 12, TB, E])
        picks = sb("picks", [P, 12, TB])
        crowd = sb("crowd", [P, 8])
        posm = sb("posm", [P, TB, E])
        comb = sb("comb", [P, TB, E])
        pcol = sb("pcol", [P, TB, 1])
        ccol = sb("ccol", [P, TB, 1])
        n_items = sb("n_items", [P, 1], I32)

        ident = consts[:, C_IDENT:C_IDENT + P]
        tri = consts[:, C_TRI:C_TRI + P]
        before = consts[:, C_BEFORE:C_BEFORE + P]
        flip = consts[:, C_FLIP:C_FLIP + P]
        iota = consts[:, C_IOTA:C_IOTA + CAP]
        desc = consts[:, C_DESC:C_DESC + E]

        bias_mask = kv_area[:, :].rearrange("p (h k) -> p h k", h=H)
        toeplitz = work[:, 0:H * WINDOW].rearrange("p (h k) -> p h k", h=H)
        hankel = o[:, :, :].rearrange("p t d -> p (t d)")
        bias_rows = work[0:H, H * WINDOW:H * WINDOW + 2 * WINDOW]
        score = [work[:, n * 1536:(n + 1) * 1536].rearrange("p (a k) -> p a k", a=GROUP) for n in range(2)]
        probT = oT[:, 0:6, :].rearrange("p t s -> p (t s)")
        kT = kv_area[:, 0:2048].rearrange("p (t s) -> p t s", t=FT)
        v_sb = kv_area[:, 2048:4096].rearrange("p (t s) -> p t s", t=TB)
        soft = [work[:, n * 768:(n + 1) * 768].rearrange("p (a k) -> p a k", a=2) for n in range(2)]
        fail = [work[:, (2 + n) * 768:(3 + n) * 768].rearrange("p (a k) -> p a k", a=2) for n in range(2)]
        stick = [oT[:, 3 * n:3 * n + 3, :].rearrange("p t s -> p (t s)").rearrange("p (a k) -> p a k", a=2) for n in range(2)]
        f_silu = [work[:, n * 512:(n + 1) * 512] for n in range(2)]
        f_hid = [work[:, (2 + n) * 512:(3 + n) * 512] for n in range(2)]
        NB = BT * CAP
        e_silu = [work[:, n * NB:(n + 1) * NB] for n in range(2)]
        e_hid = [work[:, (2 + n) * NB:(3 + n) * NB] for n in range(2)]
        w0 = 4 * NB
        gathered = work[:, w0:w0 + DT * CAP].rearrange("p (t s) -> p t s", t=DT)
        w0 += DT * CAP
        place = work[:, w0:w0 + TB * CAP].rearrange("p (t s) -> p t s", t=TB)
        w0 += TB * CAP
        weighted = work[:, w0:w0 + TB * CAP].rearrange("p (t s) -> p t s", t=TB)
        w0 += TB * CAP
        gates = work[0:CAP, w0:w0 + SEQ]
        w0 += SEQ
        assert w0 <= 3072
        y_sb = qT[0:CAP, 0:D // SEQ, :].rearrange("p t s -> p (t s)")

        bank = ctx.enter_context(nc.psum_tensor("bank", [P, 8, HALF], F32))
        bias_dram = nc.dram_tensor("bias_dram", [H, 2 * WINDOW], F32)

        ring_full = [sem(f"ring_full{n}") for n in range(RING)]
        down_used = sem("down_used")
        minus_sinks_ready = sem("minus_sinks_ready")
        final_rstd = sem("final_rstd")
        psum_full = [sem(f"psum_full{n}") for n in range(8)]
        psum_free = [sem(f"psum_free{n}") for n in range(8)]
        x_loaded = sem("x_loaded")
        consts_loaded = sem("consts_loaded")
        vectors_loaded = sem("vectors_loaded")
        rel_loaded = sem("rel_loaded")
        small_loaded = sem("small_loaded")
        final_gain_loaded = sem("final_gain_loaded")
        ones_set = sem("ones_set")
        rows_ready = sem("rows_ready")
        rows_stored = sem("rows_stored")
        hankel_loaded = sem("hankel_loaded")
        bias_ready = sem("bias_ready")
        sumsq_ready = sem("sumsq_ready")
        meansq_ready = sem("meansq_ready")
        root_ready = sem("root_ready")
        h_ready = sem("h_ready")
        k_swa_ready = sem("k_swa_ready")
        max_ready = sem("max_ready")
        exp_done = sem("exp_done")
        z_ready = sem("z_ready")
        clamped_ready = sem("clamped_ready")
        soft_ready = sem("soft_ready")
        fail_ready = sem("fail_ready")
        fail_masked = sem("fail_masked")
        stick_masked = sem("stick_masked")
        gap_ready = sem("gap_ready")
        gap_exp = sem("gap_exp")
        picks_ready = sem("picks_ready")
        items_ready = sem("items_ready")
        place_ready = sem("place_ready")
        gathered_ready = sem("gathered_ready")
        weighted_ready = sem("weighted_ready")
        act_steps = sem("act_steps")
        dve_steps = sem("dve_steps")
        trunk_done = sem("trunk_done")
        final_sumsq = sem("final_sumsq")
        final_meansq = sem("final_meansq")
        final_root = sem("final_root")
        result_ready = sem("result_ready")
        stored = sem("stored")

        def begin(pe, key, i=None):
            b, _, n = USES[key]
            if looped(key):
                pe.wait_ge(psum_free[b], i * FREES[b] + n)
            elif n > 0:
                pe.wait_ge(psum_free[b], n)
            return bank[:, b, :]

        def filled(ins, key):
            ins.then_inc(psum_full[USES[key][0]], 1)

        def full(eng, key, i=None):
            b, n, _ = USES[key]
            eng.wait_ge(psum_full[b], i * FILLS[b] + (n + 1) if looped(key) else n + 1)
            return bank[:, b, :]

        def freed(ins, key):
            ins.then_inc(psum_free[USES[key][0]], 1)

        def taken(eng, key, i=None):
            b, _, n = USES[key]
            eng.wait_ge(psum_free[b], i * FREES[b] + (n + 1) if looped(key) else n + 1)

        def arrived(eng, n, i=None):
            value = 16 * (n // RING + 1)
            if i is not None:
                value = i * (16 * MOE_LOADS // RING) + value
            eng.wait_ge(ring_full[n % RING], value)
            return ring[n % RING]

        last_reader = dict(enumerate([("q", 1), ("q", 3), "v"] + [("wo0", dh, TB - 1) for dh in range(DH)]))
        for b in range(FFN_BLOCKS):
            n = min(2 * b + 1, UNITS - 1)
            last_reader[N_FFN + 3 * b] = ("fg", n)
            last_reader[N_FFN + 3 * b + 1] = ("fu", n)
            last_reader[N_FFN + 3 * b + 2] = b + 1 if b < FFN_BLOCKS - 1 else ("fy", TB - 1, DH - 1)
        for n, key in enumerate([("q1", 1), ("q1", 3), ("k1", 1), ("k1", 3), ("v1", 0, 1), ("v1", 1, 1),
                                 ("wo1", 0, TB - 1), ("wo1", 1, TB - 1)]):
            last_reader[N_QKV1 + n] = key
        for (kind, b), k in MOE_AT.items():
            if kind == "down":
                last_reader[N_MOE + k] = FFN_BLOCKS + b if b < BLOCKS - 1 else ("y", DH - 1)
            else:
                last_reader[N_MOE + k] = (kind[0], b)

        def used(eng, n, i=None):
            key = last_reader[n]
            if isinstance(key, int):
                eng.wait_ge(down_used, key if i is None else i * (BLOCKS - 1) + key)
            else:
                full(eng, key, i)

        block = ctx.enter_context(nc.Block())

        @block.sync
        def _(sp):
            sp.dma_start(x[:, :, :], a["x"][0].rearrange("(t p) d -> p t d", p=P)).then_inc(x_loaded, 16)
            sp.dma_start(consts[:, :], a["consts"]).then_inc(consts_loaded, 16)

            def load(n, dst, src, i=None):
                if n - RING >= N_MOE:
                    used(sp, n - RING, i)
                elif i is not None and not isinstance(i, int):
                    used(sp, n - RING + MOE_LOADS, i - 1)
                elif n >= RING:
                    used(sp, n - RING)
                sp.dma_start(dst, src).then_inc(ring_full[n % RING], 16)

            def columns(n, w, c0, c1, i=None):
                load(n, ring[n % RING][:, :, 0:c1 - c0], w[:, c0:c1].rearrange("(t p) n -> p t n", p=P), i)

            def rows(n, w, r0, r1, i=None):
                t = (r1 - r0) // P
                dst = ring[n % RING][:, 0:2 * t, :].rearrange("p (t c) n -> p t (c n)", t=t)
                load(n, dst, w[r0:r1, :].rearrange("(t p) n -> p t n", p=P), i)

            w = a["swa_w_qkv"][0]
            for n in range(Q_LOADS):
                columns(n, w, n * HALF, min((n + 1) * HALF, w.shape[1]))
            for dh in range(DH):
                columns(N_WO0 + dh, a["swa_w_o"][0], dh * HALF, (dh + 1) * HALF)
            for b in range(FFN_BLOCKS):
                lo, hi = b * HALF, min((b + 1) * HALF, FFN)
                columns(N_FFN + 3 * b, a["ffn_w_gate"][0], lo, hi)
                columns(N_FFN + 3 * b + 1, a["ffn_w_up"][0], lo, hi)
                rows(N_FFN + 3 * b + 2, a["ffn_w_down"][0], lo, hi)
            for n in range(6):
                columns(N_QKV1 + n, a["sb_w_qkv"][0], n * HALF, (n + 1) * HALF)
            for dh in range(DH):
                columns(N_WO1 + dh, a["sb_w_o"][0], dh * HALF, (dh + 1) * HALF)

            def expert_loads(e, i):
                for k, (kind, b) in enumerate(MOE_ORDER):
                    lo, hi = b * HALF, (b + 1) * HALF
                    whole = a["moe_w_" + kind][0]
                    if kind == "down":
                        w = whole[bass.ds(e, 1), lo:hi, :].rearrange("o f d -> (o f) d")
                        rows(N_MOE + k, w, 0, HALF, i)
                    else:
                        w = whole[bass.ds(e, 1), :, lo:hi].rearrange("o d f -> (o d) f")
                        columns(N_MOE + k, w, 0, HALF, i)

            expert_loads(0, 0)
            with sp.Fori(1, E) as i:
                expert_loads(i, i)
            sp.wait_ge(items_ready, 1)
            items = sp.value_load(n_items[0:1, 0:1], min_val=E, max_val=PASSES * E)
            with sp.If(items > E):
                with sp.Fori(E, items, E) as before_pass:
                    with sp.Fori(0, E) as e:
                        expert_loads(e, before_pass + e)

            for tb in range(TB):
                sp.wait_ge(result_ready, tb + 1)
                sp.dma_start(a["out"][0, tb * P:(tb + 1) * P, :], h[:, tb, :]).then_inc(stored, 16)
            sp.wait_ge(stored, 16 * TB)

        @block.gpsimd
        def _(pool):
            nc.gpsimd.memset(ones[:, :], 1.0).then_inc(ones_set, 1)
            nc.gpsimd.memset(minus_ones[:, :], -1.0).then_inc(ones_set, 1)
            for n in range(4):
                taken(pool, ("toeplitz", n))
            nc.gpsimd.affine_select(out=bias_mask[:, :, WINDOW:2 * WINDOW], in_=toeplitz, compare_op=ALU.is_ge,
                                    fill=MASKED, base=0, pattern=[[0, H], [-1, WINDOW]],
                                    channel_multiplier=1).then_inc(bias_ready, 1)
            nc.gpsimd.affine_select(out=bias_mask[:, :, 0:WINDOW], in_=toeplitz, compare_op=ALU.is_gt,
                                    fill=MASKED, base=0, pattern=[[0, H], [1, WINDOW]],
                                    channel_multiplier=-1).then_inc(bias_ready, 1)

            def strictly_causal(t, done):
                for half in range(2):
                    blocks = t[:, half, :].rearrange("p (b k) -> p b k", b=3)[:, 0:3:2, :]
                    ins = nc.gpsimd.affine_select(out=blocks, in_=blocks, compare_op=ALU.is_gt, fill=0.0, base=0,
                                                  pattern=[[0, 2], [1, P]], channel_multiplier=-1)
                ins.then_inc(done, 1)

            for b in range(FT + 1):
                if b < FT:
                    pool.wait_ge(fail_ready, b + 1)
                    strictly_causal(fail[b % 2], fail_masked)
                if b >= 1:
                    for half in range(2):
                        taken(pool, ("z", b - 1, half))
                    strictly_causal(stick[(b - 1) % 2], stick_masked)

        def gain(k):
            return [0, 2 * DT, DT, 3 * DT][k]

        @block.scalar
        def _(act):
            act.dma_start(vec_rows[0:16, :], a["attn_norm"].rearrange("l (t p) -> (l t) p", p=P)).then_inc(vectors_loaded, 16)
            act.dma_start(vec_rows[16:32, :], a["ffn_norm"].rearrange("l (t p) -> (l t) p", p=P)).then_inc(vectors_loaded, 16)
            act.dma_start(vec_rows[32:42, :], a["swa_b_qkv"].rearrange("l (t p) -> (l t) p", p=P)).then_inc(vectors_loaded, 16)
            act.dma_start(rel[:, :], a["rel_bias"]).then_inc(rel_loaded, 16)
            act.dma_start(onehot[:, :], a["onehot"]).then_inc(rel_loaded, 16)
            act.dma_start(v_bias[:, :], a["swa_b_qkv"][:, (H + KV) * HD:]).then_inc(small_loaded, 16)
            act.dma_start(sinks[:, :], a["swa_sinks"].to_broadcast([P, H])).then_inc(small_loaded, 16)
            act.dma_start(router[:, :, :], a["moe_router"][0].rearrange("(t p) e -> p t e", p=P)).then_inc(small_loaded, 16)
            act.dma_start(final_gain[:, :], a["final_norm"].rearrange("(o d) -> o d", o=1).to_broadcast([P, D])).then_inc(final_gain_loaded, 16)

            steps = Steps(act, act_steps)

            def norm(k, x_from):
                if k == 0:
                    act.wait_ge(x_loaded, 16)
                for key in x_from:
                    taken(act, key)
                for tb in range(TB):
                    nc.scalar.activation(h[:, tb, :], x[:, tb, :], ACT.Square,
                                         accum_out=sumsq[:, tb:tb + 1]).then_inc(sumsq_ready, 1)
                act.wait_ge(meansq_ready, k + 1)
                nc.scalar.activation(root[:, :], meansq[:, :], ACT.Sqrt).then_inc(root_ready, 1)

            def transposed_h(k):
                for j in (1, 3):
                    b = full(act, (f"hT{k}", j))
                    for s in range(2):
                        t = 2 * j + s
                        last = nc.scalar.activation(hT[:, t, :], b[:, s * SEQ:(s + 1) * SEQ], ACT.Copy,
                                                    scale=vec[:, gain(k) + t:gain(k) + t + 1])
                    freed(last, (f"hT{k}", j))

            def transposed_o(k):
                for j in (1, 3):
                    b = full(act, (f"oT{k}", j))
                    freed(nc.scalar.copy(oT[:, 2 * j:2 * j + 2, :].rearrange("p t s -> p (t s)"), b), (f"oT{k}", j))

            b = full(act, "bias rows")
            freed(nc.scalar.copy(bias_rows, b[0:H, 0:2 * WINDOW]), "bias rows")
            taken(act, "bias rows")
            act.dma_start(bias_dram.ap(), bias_rows).then_inc(rows_stored, 16)
            norm(0, [])
            act.wait_ge(rows_stored, 16)
            act.dma_start(hankel.rearrange("p (h k) -> p h k", h=H),
                          bass.AP(bias_dram, 1, [[1, P], [2 * WINDOW, H], [1, WINDOW]])).then_inc(hankel_loaded, 16)
            taken(act, "vectors")
            transposed_h(0)
            b = full(act, "v")
            freed(nc.scalar.copy(v_swa[:, :, :].rearrange("p t s -> p (t s)"), b[:, 0:TB * KV * HD]), "v")
            for n in range(4):
                b = full(act, ("toeplitz", n))
                freed(nc.scalar.copy(work[:, n * HALF:(n + 1) * HALF], b), ("toeplitz", n))

            for g in range(H // GROUP + 1):
                if g < H // GROUP:
                    s, m = score[g % 2], g % 2
                    act.wait_ge(max_ready, g + 1)
                    for n in range(GROUP):
                        for tb, c0, c1 in ((1, 0, 2 * P), (0, 2 * P, 3 * P)):
                            nc.scalar.activation(s[:, n, c0:c1], s[:, n, c0:c1], ACT.Exp,
                                                 bias=shift[:, m, tb, n:n + 1],
                                                 accum_out=row_sum[:, m, tb, n:n + 1])
                    nc.scalar.activation(sink_exp[:, m, :, :], sink_gap[:, m, :, :], ACT.Exp).then_inc(exp_done, 1)
                if g >= 1:
                    if g >= 2:
                        full(act, ("o", g - 2))
                    for t in range(3):
                        b = full(act, ("pT", g - 1, t))
                        freed(nc.scalar.copy(probT[:, t * HALF:(t + 1) * HALF], b), ("pT", g - 1, t))
            transposed_o(0)
            norm(1, [("wo0", dh, tb) for dh in range(DH) for tb in range(TB)])
            transposed_h(1)

            for n in range(UNITS):
                b = full(act, ("fg", n))
                freed(nc.scalar.activation(f_silu[n % 2], b, ACT.Silu), ("fg", n))
            norm(2, [("fy", tb, dh) for tb in range(TB) for dh in range(DH)])
            transposed_h(2)
            for j in range(FT // 2):
                b = full(act, ("k1", j))
                freed(nc.scalar.copy(kT[:, 2 * j:2 * j + 2, :].rearrange("p t s -> p (t s)"), b), ("k1", j))

            for b in range(FT + 1):
                if b < FT:
                    act.wait_ge(clamped_ready, b + 1)
                    steps.mark(nc.scalar.activation(soft[b % 2], soft[b % 2], ACT.Exp))
                    steps.settle()
                    nc.scalar.activation(soft[b % 2], soft[b % 2], ACT.Ln, bias=1.0).then_inc(soft_ready, 1)
                if b >= 1:
                    c = b - 1
                    if c >= 2 and c % 2 == 0:
                        full(act, ("so", c // 2 - 1))
                    for half in range(2):
                        p = full(act, ("z", c, half))
                        freed(nc.scalar.activation(stick[c % 2][:, half, :], p[:, 0:3 * P], ACT.Exp), ("z", c, half))
            transposed_o(1)
            norm(3, [("wo1", dh, tb) for dh in range(DH) for tb in range(TB)])
            transposed_h(3)
            act.wait_ge(gap_ready, 1)
            nc.scalar.activation(picks[:, 5, :], picks[:, 4, :], ACT.Exp).then_inc(gap_exp, 1)

            act.wait_ge(items_ready, 1)
            items = act.value_load(n_items[0:1, 0:1], min_val=E, max_val=PASSES * E)
            with act.Fori(0, items) as i:
                for b in range(BLOCKS):
                    p = full(act, ("g", b), i)
                    freed(nc.scalar.activation(e_silu[b % 2], p[:, 0:NB], ACT.Silu), ("g", b))
                    if b == 0:
                        p = full(act, "gates", i)
                        freed(nc.scalar.copy(gates, p[0:CAP, 0:SEQ]), "gates")
                for dh in range(DH):
                    p = full(act, ("y", dh), i)
                    freed(nc.scalar.copy(y_sb[:, dh * HALF:(dh + 1) * HALF], p[0:CAP, :]), ("y", dh))

            act.wait_ge(trunk_done, 1)
            for tb in range(TB):
                nc.scalar.activation(h[:, tb, :], x[:, tb, :], ACT.Square,
                                     accum_out=sumsq[:, tb:tb + 1]).then_inc(final_sumsq, 1)
            act.wait_ge(final_meansq, 1)
            nc.scalar.activation(root[:, :], meansq[:, :], ACT.Sqrt).then_inc(final_root, 1)

        @block.vector
        def _(dve):
            V = nc.vector
            steps = Steps(dve, dve_steps)

            b = full(dve, "vectors")
            freed(V.tensor_copy(vec[:, :], b[:, 0:42]), "vectors")
            dve.wait_ge(small_loaded, 48)
            V.tensor_scalar(minus_sinks[:, :].rearrange("p (g f j) -> p g f j", g=H // GROUP, f=2),
                            sinks[:, :].rearrange("p (g j f) -> p g f j", g=H // GROUP, f=2),
                            -1.0, None, ALU.mult).then_inc(minus_sinks_ready, 1)
            taken(dve, "vectors")

            def norm(k):
                dve.wait_ge(sumsq_ready, TB * (k + 1))
                V.tensor_scalar(meansq[:, :], sumsq[:, :], 1.0 / D, EPS, ALU.mult, ALU.add).then_inc(meansq_ready, 1)
                dve.wait_ge(root_ready, k + 1)
                steps.mark(V.reciprocal(rstd[:, :], root[:, :]))
                steps.settle()
                for tb in range(TB):
                    V.tensor_scalar(h[:, tb, :], x[:, tb, :], rstd[:, tb:tb + 1], None, ALU.mult).then_inc(h_ready, 1)

            def transposed_h(k):
                for j in (0, 2):
                    b = full(dve, (f"hT{k}", j))
                    g = vec[:, gain(k) + 2 * j:gain(k) + 2 * j + 2].unsqueeze(2).to_broadcast([P, 2, SEQ])
                    freed(V.tensor_tensor(hT[:, 2 * j:2 * j + 2, :], b.rearrange("p (t s) -> p t s", t=2), g,
                                          ALU.mult), (f"hT{k}", j))

            def transposed_o(k):
                for j in (0, 2):
                    b = full(dve, (f"oT{k}", j))
                    freed(V.tensor_copy(oT[:, 2 * j:2 * j + 2, :].rearrange("p t s -> p (t s)"), b), (f"oT{k}", j))

            def add_to_x(key, tb, dh, i=None):
                b = full(dve, key, i)
                part = x[:, tb, dh * HALF:(dh + 1) * HALF]
                ins = V.tensor_tensor(part, part, b, ALU.add)
                freed(ins, key)
                return ins

            norm(0)
            transposed_h(0)

            for j in range(FT // 2):
                b = full(dve, ("q", j))
                for s in range(2):
                    t = 2 * j + s
                    ins = V.tensor_scalar(qT[:, t, :], b[:, s * SEQ:(s + 1) * SEQ],
                                          vec[:, 4 * DT + t:4 * DT + t + 1], SCALE, ALU.add, ALU.mult)
                freed(ins, ("q", j))
            b = full(dve, "k")
            freed(V.tensor_scalar(k_swa[:, :], b[:, 0:SEQ], vec[:, 4 * DT + FT:4 * DT + FT + 1], None, ALU.add), "k")
            taken(dve, "k")
            for kv in range(KV):
                for half in range(2):
                    ins = V.tensor_copy(kT_swa[half * HD:(half + 1) * HD, kv, :], k_swa[kv * HD:(kv + 1) * HD, :])
            ins.then_inc(k_swa_ready, 1)

            dve.wait_ge(bias_ready, 2)
            dve.wait_ge(minus_sinks_ready, 1)
            for g in range(H // GROUP + 2):
                if g < H // GROUP:
                    s, m = score[g % 2], g % 2
                    for half in range(2):
                        first = GROUP * g + half
                        for kind, c0, c1 in (("s1", 0, 2 * P), ("s0", 2 * P, 3 * P)):
                            b = full(dve, (kind, g, half))
                            n = c1 - c0
                            freed(V.tensor_tensor(s[:, 2 * half:2 * half + 2, c0:c1],
                                                  b[:, 0:2 * n].rearrange("p (j k) -> p j k", j=2),
                                                  bias_mask[:, first:first + 3:2, 2 * P - n:2 * P], ALU.add),
                                  (kind, g, half))
                    for half in range(2):
                        for kind in ("s1", "s0"):
                            taken(dve, (kind, g, half))
                    V.tensor_reduce(peak[:, m, 1, :], s[:, :, 0:2 * P], axis=AX.X, op=ALU.max)
                    steps.mark(V.tensor_reduce(peak[:, m, 0, :], s[:, :, 2 * P:3 * P], axis=AX.X, op=ALU.max))
                    steps.settle()
                    ms = minus_sinks[:, GROUP * g:GROUP * (g + 1)].unsqueeze(1).to_broadcast([P, TB, GROUP])
                    steps.mark(V.scalar_tensor_tensor(shift[:, m, :, :], peak[:, m, :, :], -1.0, ms, ALU.mult, ALU.min))
                    steps.settle()
                    V.tensor_tensor(sink_gap[:, m, :, :], shift[:, m, :, :], ms, ALU.subtract).then_inc(max_ready, 1)
                if 1 <= g <= H // GROUP:
                    m = (g - 1) % 2
                    dve.wait_ge(exp_done, g)
                    steps.mark(V.tensor_tensor(total[:, m, :, :], row_sum[:, m, :, :], sink_exp[:, m, :, :], ALU.add))
                    steps.settle()
                    steps.mark(V.reciprocal(inverse[:, m, :, :], total[:, m, :, :]))
                if g >= 2:
                    m = g % 2
                    b = full(dve, ("o", g - 2))
                    steps.settle()
                    for tb in range(TB):
                        inv = inverse[:, m, tb, :].rearrange("p (f j) -> p f j", f=2).unsqueeze(3).to_broadcast([P, 2, 2, HD])
                        w = GROUP * HD
                        ins = V.tensor_tensor(
                            o[:, tb, (g - 2) * w:(g - 1) * w].rearrange("p (j f d) -> p f j d", f=2, d=HD),
                            b[:, tb * w:(tb + 1) * w].rearrange("p (f j d) -> p f j d", f=2, d=HD), inv, ALU.mult)
                    freed(ins, ("o", g - 2))
            transposed_o(0)
            for dh in range(DH):
                for tb in range(TB):
                    add_to_x(("wo0", dh, tb), tb, dh)
            norm(1)
            transposed_h(1)

            for n in range(UNITS):
                b = full(dve, ("fu", n))
                taken(dve, ("fg", n))
                freed(V.tensor_tensor(f_hid[n % 2], f_silu[n % 2], b, ALU.mult), ("fu", n))
            for tb in range(TB):
                for dh in range(DH):
                    add_to_x(("fy", tb, dh), tb, dh)
            norm(2)
            transposed_h(2)

            for j in range(FT // 2):
                b = full(dve, ("q1", j))
                freed(V.tensor_scalar(qT[:, 2 * j:2 * j + 2, :].rearrange("p t s -> p (t s)"), b, SCALE, None,
                                      ALU.mult), ("q1", j))
            for vh in range(2):
                for tb in range(TB):
                    b = full(dve, ("v1", vh, tb))
                    freed(V.tensor_copy(v_sb[:, tb, vh * HALF:(vh + 1) * HALF], b), ("v1", vh, tb))
            for b in range(FT + 3):
                if b < FT:
                    lo = 2 * b % 6
                    dve.wait_ge(z_ready, b + 1)
                    V.tensor_scalar(soft[b % 2], bank[:, lo:lo + 2, 0:3 * P], SOFT_TOP, None, ALU.min).then_inc(clamped_ready, 1)
                if 1 <= b <= FT:
                    c = b - 1
                    lo = 2 * c % 6
                    dve.wait_ge(soft_ready, b)
                    if c >= 2:
                        for half in range(2):
                            full(dve, ("z", c - 2, half))
                    V.tensor_tensor(fail[c % 2], bank[:, lo:lo + 2, 0:3 * P], soft[c % 2], ALU.max).then_inc(fail_ready, 1)
                if b >= 4 and b % 2 == 0:
                    n, w = b // 2 - 2, GROUP * HD
                    p = full(dve, ("so", n))
                    freed(V.tensor_copy(o[:, :, n * w:(n + 1) * w], p.rearrange("p (t c) -> p t c", t=TB)), ("so", n))
            transposed_o(1)
            for dh in range(DH):
                for tb in range(TB):
                    add_to_x(("wo1", dh, tb), tb, dh)
            norm(3)
            transposed_h(3)

            def link(ins):
                steps.mark(ins)
                steps.settle()

            def wide(v):
                return v.unsqueeze(2).to_broadcast([P, TB, E])

            dsc = desc.unsqueeze(1).to_broadcast([P, TB, E])
            R = [route[:, n, :, :] for n in range(12)]
            K = [picks[:, n, :] for n in range(12)]
            logits = R[0]
            b = full(dve, "logits")
            freed(V.tensor_copy(logits, b[:, 0:TB * E].rearrange("p (t e) -> p t e", t=TB)), "logits")
            taken(dve, "logits")

            def largest(values, top, first, spare):
                link(V.tensor_reduce(top, values, axis=AX.X, op=ALU.max))
                link(V.tensor_tensor(spare[0], values, wide(top), ALU.is_equal))
                link(V.tensor_tensor(spare[0], spare[0], dsc, ALU.mult))
                link(V.tensor_reduce(spare[1], spare[0], axis=AX.X, op=ALU.max))
                link(V.tensor_tensor(first, spare[0], wide(spare[1]), ALU.is_equal))

            largest(logits, K[0], R[1], (R[2], K[1]))
            link(V.scalar_tensor_tensor(R[3], R[1], -3e38, logits, ALU.mult, ALU.add))
            largest(R[3], K[2], R[4], (R[5], K[3]))
            V.tensor_tensor(K[4], K[2], K[0], ALU.subtract).then_inc(gap_ready, 1)
            V.tensor_tensor(R[6], R[1], R[4], ALU.add).then_inc(picks_ready, 1)
            dve.wait_ge(gap_exp, 1)
            link(V.tensor_scalar(K[6], K[5], 1.0, None, ALU.add))
            link(V.reciprocal(K[7], K[6]))
            link(V.tensor_tensor(K[8], K[5], K[7], ALU.mult))
            link(V.tensor_tensor(R[7], R[1], wide(K[7]), ALU.mult))
            link(V.tensor_tensor(R[8], R[4], wide(K[8]), ALU.mult))
            link(V.tensor_tensor(comb[:, :, :], R[7], R[8], ALU.add))
            b = full(dve, "places")
            link(V.scalar_tensor_tensor(R[9], b[:, 0:TB * E].rearrange("p (t e) -> p t e", t=TB), 1.0, R[6],
                                        ALU.add, ALU.mult))
            link(V.tensor_scalar(posm[:, :, :], R[9], -1.0, None, ALU.add))
            ins = V.tensor_reduce(crowd[:, 0:1], b[:, TB * E:(TB + 1) * E], axis=AX.X, op=ALU.max)
            freed(ins, "places")
            taken(dve, "places")
            for n in range(1, PASSES):
                V.tensor_scalar(crowd[:, n:n + 1], crowd[:, 0:1], float(n * CAP), float(E), ALU.is_gt, ALU.mult)
            link(V.memset(crowd[:, PASSES:PASSES + 1], float(E)))
            link(V.tensor_reduce(crowd[:, PASSES + 1:PASSES + 2], crowd[:, 1:PASSES + 1], axis=AX.X, op=ALU.add))
            V.tensor_copy(n_items[:, :], crowd[:, PASSES + 1:PASSES + 2]).then_inc(items_ready, 1)

            def choose(e):
                steps.mark(V.tensor_copy(pcol[:, :, :], posm[:, :, e]))
                steps.mark(V.tensor_copy(ccol[:, :, :], comb[:, :, e]))
                steps.settle()
                for tb in range(TB):
                    ins = V.tensor_scalar(place[:, tb, :], iota, pcol[:, tb, :], None, ALU.is_equal)
                ins.then_inc(place_ready, 1)

            def take_gathered(name, i=None):
                for q in range(2):
                    b = full(dve, (name, q), i)
                    g = vec[:, gain(3) + 4 * q:gain(3) + 4 * q + 4].unsqueeze(2).to_broadcast([P, 4, CAP])
                    V.tensor_tensor(gathered[:, 4 * q:4 * q + 4, :],
                                    b[:, 0:4 * CAP].rearrange("p (t s) -> p t s", t=4), g,
                                    ALU.mult).then_inc(gathered_ready, 1)

            choose(slice(0, 1))
            take_gathered("first gather")
            dve.wait_ge(items_ready, 1)
            items = dve.value_load(n_items[0:1, 0:1], min_val=E, max_val=PASSES * E)
            with dve.Fori(0, items) as i:
                steps.loop(i, 3)
                e, e_next = i & (E - 1), (i + 1) & (E - 1)
                for tb in range(TB):
                    ins = V.tensor_scalar(weighted[:, tb, :], iota, pcol[:, tb, :], ccol[:, tb, :],
                                          ALU.is_equal, ALU.mult)
                ins.then_inc(weighted_ready, 1)
                for b in range(BLOCKS):
                    p = full(dve, ("u", b), i)
                    taken(dve, ("g", b), i)
                    freed(V.tensor_tensor(e_hid[b % 2], e_silu[b % 2], p[:, 0:NB], ALU.mult), ("u", b))
                    if b == 0:
                        dve.wait_ge(weighted_ready, i + 1)
                        here = posm[:, :, bass.ds(e, 1)]
                        steps.mark(V.tensor_scalar(here, here, -float(CAP), None, ALU.add))
                        choose(bass.ds(e_next, 1))
                take_gathered("gather", i)
                for n in range(TB * DH):
                    add_to_x(("scatter", n), n // DH, n % DH, i)
                steps.end()

            V.memset(crowd[:, 0:1], 0.0).then_inc(trunk_done, 1)
            dve.wait_ge(final_sumsq, TB)
            V.tensor_scalar(meansq[:, :], sumsq[:, :], 1.0 / D, EPS, ALU.mult, ALU.add).then_inc(final_meansq, 1)
            dve.wait_ge(final_root, 1)
            dve.wait_ge(final_gain_loaded, 16)
            V.reciprocal(rstd[:, :], root[:, :]).then_inc(final_rstd, 1)
            dve.wait_ge(final_rstd, 1)
            for tb in range(TB):
                V.scalar_tensor_tensor(h[:, tb, :], x[:, tb, :], rstd[:, tb:tb + 1], final_gain[:, :],
                                       ALU.mult, ALU.mult).then_inc(result_ready, 1)

        @block.tensor
        def _(pe):
            def mm(out, lhsT, rhs, start, stop, **kw):
                return nc.tensor.matmul(out, lhsT, rhs, start=start, stop=stop, **kw)

            def release(ins):
                ins.then_inc(ring_released, 1)

            pe.wait_ge(vectors_loaded, 48)
            pe.wait_ge(consts_loaded, 16)
            b = begin(pe, "vectors")
            filled(nc.tensor.transpose(b[:, 0:42], vec_rows[:, :], ident[0:42, 0:42]), "vectors")
            pe.wait_ge(rel_loaded, 32)
            b = begin(pe, "bias rows")
            filled(mm(b[0:H, 0:2 * WINDOW], rel[:, :], onehot[:, :], True, True), "bias rows")

            def transposed(src, name, ready=None):
                for tb in range(TB):
                    if ready is not None:
                        ready(tb)
                    for j in range(4):
                        b = begin(pe, (name, j)) if tb == 0 else bank[:, USES[(name, j)][0], :]
                        for s in range(2):
                            t = 2 * j + s
                            ins = nc.tensor.transpose(b[:, s * SEQ + tb * P:s * SEQ + (tb + 1) * P],
                                                      src[:, tb, t * P:(t + 1) * P], ident)
                        if tb == TB - 1:
                            filled(ins, (name, j))

            def transposed_h(k):
                transposed(h, f"hT{k}", lambda tb: pe.wait_ge(h_ready, TB * k + tb + 1))
                for j in range(4):
                    taken(pe, (f"hT{k}", j))

            def transposed_o(k, last):
                for key in last:
                    taken(pe, key)
                transposed(o, f"oT{k}")
                for j in range(4):
                    taken(pe, (f"oT{k}", j))

            def project(out, w, lhs_cols, tokens):
                for t in range(DT):
                    ins = mm(out, w[:, t, lhs_cols], hT[:, t, tokens], t == 0, t == DT - 1)
                return ins

            def output_projection(k, n0):
                for dh in range(DH):
                    w = arrived(pe, n0 + dh)
                    for tb in range(TB):
                        b = begin(pe, (f"wo{k}", dh, tb))
                        for t in range(FT):
                            ins = mm(b, oT[:, t, tb * P:(tb + 1) * P], w[:, t, :], t == 0, t == FT - 1)
                        filled(ins, (f"wo{k}", dh, tb))

            def by_rows(slot):
                return slot[:, :, :].rearrange("p (t c) n -> p t (c n)", c=DT // BT)

            every = slice(0, SEQ)

            def features(name, n0):
                for j in range(FT // 2):
                    w = arrived(pe, n0 + j // 2)
                    b = begin(pe, (name, j))
                    for s in range(2):
                        c = (2 * j + s) % BT * P
                        ins = project(b[:, s * SEQ:(s + 1) * SEQ], w, slice(c, c + P), every)
                    filled(ins, (name, j))

            transposed_h(0)
            features("q", 0)
            w = arrived(pe, 2)
            filled(project(begin(pe, "k")[:, 0:SEQ], w, slice(0, P), every), "k")
            pe.wait_ge(small_loaded, 48)
            pe.wait_ge(ones_set, 2)
            b = begin(pe, "v")
            for tb in range(TB):
                out = b[:, tb * P:(tb + 1) * P]
                for t in range(DT):
                    mm(out, hT[:, t, tb * P:(tb + 1) * P], w[:, t, P:2 * P], t == 0, False)
                ins = mm(out, ones[0:1, :], v_bias[:, :], False, True)
            filled(ins, "v")
            pe.wait_ge(hankel_loaded, 16)
            for n in range(4):
                filled(mm(begin(pe, ("toeplitz", n)), flip, hankel[:, n * HALF:(n + 1) * HALF], True, True), ("toeplitz", n))

            def swa_scores(g):
                kv = g * GROUP // (H // KV)
                taken(pe, ("q", g))
                for half in range(2):
                    p0 = half * HD
                    for kind, tb, n in (("s1", 1, 2 * P), ("s0", 0, P)):
                        b = begin(pe, (kind, g, half))
                        for j in range(2):
                            ins = mm(b[:, j * n:(j + 1) * n], qT[p0:p0 + HD, 2 * g + j, tb * P:(tb + 1) * P],
                                     kT_swa[p0:p0 + HD, kv, 0:n], True, True)
                        filled(ins, (kind, g, half))

            def swa_transpose(g):
                s = score[g % 2].rearrange("p a k -> p (a k)")
                pe.wait_ge(exp_done, g + 1)
                for t in range(3):
                    b = begin(pe, ("pT", g, t))
                    for c in range(4):
                        ins = nc.tensor.transpose(b[:, c * P:(c + 1) * P], s[:, (4 * t + c) * P:(4 * t + c + 1) * P], ident)
                    filled(ins, ("pT", g, t))

            def swa_values(g):
                kv = g * GROUP // (H // KV)
                for t in range(3):
                    taken(pe, ("pT", g, t))
                b = begin(pe, ("o", g))
                for tb, parts in ((0, ((2, 0),)), (1, ((0, 0), (1, 1)))):
                    for n in range(GROUP):
                        out = b[:, (tb * GROUP + n) * HD:(tb * GROUP + n + 1) * HD]
                        for c, kb in parts:
                            ins = mm(out, probT[:, (3 * n + c) * P:(3 * n + c + 1) * P],
                                     v_swa[:, kb, kv * HD:(kv + 1) * HD], c == parts[0][0], c == parts[-1][0])
                filled(ins, ("o", g))

            pe.wait_ge(k_swa_ready, 1)
            taken(pe, "v")
            for g in range(H // GROUP + 2):
                if g < H // GROUP:
                    swa_scores(g)
                if 1 <= g <= H // GROUP:
                    swa_transpose(g - 1)
                if g >= 2:
                    swa_values(g - 2)
            transposed_o(0, [("o", g) for g in range(H // GROUP)])
            output_projection(0, N_WO0)

            transposed_h(1)

            def ffn_gate_up(n):
                for kind, k in (("fg", 0), ("fu", 1)):
                    w = arrived(pe, N_FFN + 3 * (n // 2) + k)
                    b = begin(pe, (kind, n))
                    for s in range(2):
                        c = (2 * (n % 2) + s) * P
                        ins = project(b[:, s * SEQ:(s + 1) * SEQ], w, slice(c, c + P), every)
                    filled(ins, (kind, n))

            def ffn_down(n):
                w = by_rows(arrived(pe, N_FFN + 3 * (n // 2) + 2))
                taken(pe, ("fu", n))
                for s in range(2):
                    for tb in range(TB):
                        for dh in range(DH):
                            if n == 0 and s == 0:
                                begin(pe, ("fy", tb, dh))
                            last = n == UNITS - 1 and s == 1
                            ins = mm(bank[:, USES[("fy", tb, dh)][0], :],
                                     f_hid[n % 2][:, s * SEQ + tb * P:s * SEQ + (tb + 1) * P],
                                     w[:, 2 * (n % 2) + s, dh * HALF:(dh + 1) * HALF], n == 0 and s == 0, last)
                            if last:
                                filled(ins, ("fy", tb, dh))
                if n % 2 == 1:
                    ins.then_inc(down_used, 1)

            for n in range(UNITS + 1):
                if n < UNITS:
                    ffn_gate_up(n)
                if n >= 1:
                    ffn_down(n - 1)

            transposed_h(2)
            features("q1", N_QKV1)
            features("k1", N_QKV1 + 2)
            for vh in range(2):
                w = arrived(pe, N_QKV1 + 4 + vh)
                for tb in range(TB):
                    b = begin(pe, ("v1", vh, tb))
                    for t in range(DT):
                        ins = mm(b, hT[:, t, tb * P:(tb + 1) * P], w[:, t, :], t == 0, t == DT - 1)
                    filled(ins, ("v1", vh, tb))

            def sb_scores(n):
                taken(pe, ("q1", n // 2))
                taken(pe, ("k1", n // 2))
                for half in range(2):
                    p0 = half * HD
                    b = begin(pe, ("z", n, half))
                    mm(b[:, 0:SEQ], kT[p0:p0 + HD, n, 0:P], qT[p0:p0 + HD, n, :], True, False, skip_group_check=True)
                    ins = mm(b[:, SEQ:SEQ + P], kT[p0:p0 + HD, n, P:SEQ], qT[p0:p0 + HD, n, P:SEQ], False, False,
                             skip_group_check=True)
                ins.then_inc(z_ready, 1)

            def sb_sums(n):
                pe.wait_ge(fail_masked, n + 1)
                for half in range(2):
                    b = bank[:, USES[("z", n, half)][0], :]
                    f = fail[n % 2][:, half, :]
                    mm(b[:, 0:SEQ], tri, f[:, 0:SEQ], False, False, skip_group_check=True)
                    mm(b[:, P:SEQ], minus_ones[:, :], f[:, SEQ:SEQ + P], False, False, skip_group_check=True)
                    ins = mm(b[:, SEQ:SEQ + P], tri, f[:, SEQ:SEQ + P], False, True, skip_group_check=True)
                    filled(ins, ("z", n, half))

            def sb_values(n):
                if n == 0:
                    for vh in range(2):
                        for tb in range(TB):
                            taken(pe, ("v1", vh, tb))
                pe.wait_ge(stick_masked, n + 1)
                key = ("so", n // 2)
                b = begin(pe, key) if n % 2 == 0 else bank[:, USES[key][0], :]
                for half in range(2):
                    head = 2 * n + half
                    s = stick[n % 2][:, half, :]
                    vc = slice(head * HD, (head + 1) * HD)
                    for tb, parts in ((0, ((0, 0),)), (1, ((P, 0), (SEQ, 1)))):
                        c0 = tb * GROUP * HD + head % GROUP * HD
                        for m, (c, kb) in enumerate(parts):
                            ins = mm(b[:, c0:c0 + HD], s[:, c:c + P], v_sb[:, kb, vc], m == 0, m == len(parts) - 1)
                if n % 2 == 1:
                    filled(ins, key)

            for n in range(FT + 2):
                if n < FT:
                    sb_scores(n)
                if 1 <= n <= FT:
                    sb_sums(n - 1)
                if n >= 2:
                    sb_values(n - 2)
            transposed_o(1, [("so", n) for n in range(FT // 2)])
            output_projection(1, N_WO1)

            transposed_h(3)
            b = begin(pe, "logits")
            for tb in range(TB):
                for t in range(DT):
                    ins = mm(b[:, tb * E:(tb + 1) * E], hT[:, t, tb * P:(tb + 1) * P], router[:, t, :], t == 0, t == DT - 1)
            filled(ins, "logits")
            pe.wait_ge(picks_ready, 1)
            chosen = route[:, 6, :, :]
            b = begin(pe, "places")
            mm(b[:, 0:E], before, chosen[:, 0, :], True, True)
            mm(b[:, E:2 * E], before, chosen[:, 1, :], True, False)
            mm(b[:, E:2 * E], ones[:, :], chosen[:, 0, :], False, True)
            mm(b[:, 2 * E:3 * E], ones[:, :], chosen[:, 0, :], True, False)
            filled(mm(b[:, 2 * E:3 * E], ones[:, :], chosen[:, 1, :], False, True), "places")

            def gather(name, i=None):
                for q in range(2):
                    b = begin(pe, (name, q), i)
                    for n in range(4):
                        for tb in range(TB):
                            t = 4 * q + n
                            ins = mm(b[:, n * CAP:(n + 1) * CAP], h[:, tb, t * P:(t + 1) * P], place[:, tb, :],
                                     tb == 0, tb == TB - 1)
                    filled(ins, (name, q))

            def expert_gate_up(b, i):
                for kind in ("gate", "up"):
                    key = (kind[0], b)
                    w = arrived(pe, N_MOE + MOE_AT[(kind, b)], i)
                    out = begin(pe, key, i)
                    for s in range(BT):
                        for t in range(DT):
                            ins = mm(out[:, s * CAP:(s + 1) * CAP], w[:, t, s * P:(s + 1) * P], gathered[:, t, :],
                                     t == 0, t == DT - 1)
                    filled(ins, key)

            def expert_down(b, i):
                w = by_rows(arrived(pe, N_MOE + MOE_AT[("down", b)], i))
                taken(pe, ("u", b), i)
                for s in range(BT):
                    for dh in range(DH):
                        if b == 0 and s == 0:
                            begin(pe, ("y", dh), i)
                        last = b == BLOCKS - 1 and s == BT - 1
                        ins = mm(bank[0:CAP, USES[("y", dh)][0], :], e_hid[b % 2][:, s * CAP:(s + 1) * CAP],
                                 w[:, s, dh * HALF:(dh + 1) * HALF], b == 0 and s == 0, last)
                        if last:
                            filled(ins, ("y", dh))
                if b < BLOCKS - 1:
                    ins.then_inc(down_used, 1)

            pe.wait_ge(place_ready, 1)
            gather("first gather")
            pe.wait_ge(items_ready, 1)
            items = pe.value_load(n_items[0:1, 0:1], min_val=E, max_val=PASSES * E)
            with pe.Fori(0, items) as i:
                pe.wait_ge(gathered_ready, i * 2 + 2)
                for b in range(BLOCKS):
                    expert_gate_up(b, i)
                    if b == 0:
                        pe.wait_ge(weighted_ready, i + 1)
                        out = begin(pe, "gates", i)
                        for tb in range(TB):
                            ins = nc.tensor.transpose(out[0:CAP, tb * P:(tb + 1) * P], weighted[:, tb, :], ident)
                        filled(ins, "gates")
                    elif b < BLOCKS - 1:
                        expert_down(b - 1, i)
                pe.wait_ge(place_ready, i + 2)
                gather("gather", i)
                expert_down(BLOCKS - 2, i)
                expert_down(BLOCKS - 1, i)
                pe.wait_ge(gathered_ready, i * 2 + 4)
                taken(pe, "gates", i)
                for dh in range(DH):
                    taken(pe, ("y", dh), i)
                for n in range(TB * DH):
                    tb, dh = n // DH, n % DH
                    out = begin(pe, ("scatter", n), i)
                    filled(mm(out, gates[:, tb * P:(tb + 1) * P], y_sb[:, dh * HALF:(dh + 1) * HALF], True, True),
                           ("scatter", n))


INPUTS = ["x", "rel_bias", "attn_norm", "ffn_norm", "final_norm", "swa_w_qkv", "swa_b_qkv", "swa_sinks", "swa_w_o",
          "sb_w_qkv", "sb_w_o", "ffn_w_gate", "ffn_w_up", "ffn_w_down", "moe_router", "moe_w_gate", "moe_w_up",
          "moe_w_down"]


def kernel(**inputs):
    import concourse.bacc as bacc
    from concourse.bass_utils import run_bass_kernel_spmd

    nc = bacc.Bacc("TRN2", target_bir_lowering=False, num_devices=1)
    arrays = {name: np.ascontiguousarray(inputs[name]) for name in INPUTS}
    arrays["consts"] = constants()
    arrays["onehot"] = bucket_rows()
    a = {name: nc.dram_tensor(f"in_{name}", v.shape, F32, kind="ExternalInput").ap() for name, v in arrays.items()}
    a["out"] = nc.dram_tensor("result", (1, SEQ, D), F32, kind="ExternalOutput").ap()
    build(nc, a)
    result = run_bass_kernel_spmd(nc, [{f"in_{name}": v for name, v in arrays.items()}], core_ids=[0])
    return result.results[0]["result"]
```

```python
from contextlib import ExitStack

import numpy as np
import concourse.bass as bass
from concourse import mybir

F32 = mybir.dt.float32
F32R = mybir.dt.float32r
I32 = mybir.dt.int32
ALU = mybir.AluOpType
ACT = mybir.ActivationFunctionType
AX = mybir.AxisListType

P = 128
SEQ, D = 256, 1024
TB = SEQ // P
DT = D // P
HALF = 512
DH = D // HALF
H, HD = 16, 64
FT = H * HD // P
KV = 2
WINDOW = 128
GROUP = 4
BUCKETS, MAX_DIST = 32, 128
FFN = 2816
FFN_TILES = FFN // P
E, EDIM = 8, 3584
BLOCKS = EDIM // HALF
BT = HALF // P
CAP = P
PASSES = -(-SEQ // CAP)
EPS = 1e-6
SCALE = HD ** -0.5
MASKED = -1e30
SOFT_TOP = 30.0

HALF_T = DT // 2
RAW = 6
SPLIT = 3
FFN_BLOCKS = -(-FFN_TILES // BT)


def block_order(blocks):
    order = []
    for b in range(blocks):
        order += [("gate", b), ("up", b)] + ([("down", b - 1)] if b else [])
    return order + [("down", blocks - 1)]


def unit_ends():
    ends, at = [], {}

    def add(name, *keys):
        at[name] = len(ends)
        ends.extend(keys)

    add("qkv0", None, ("q", 1), None, ("q", 3), None, "v")
    add("wo0", None, ("wo0", 0, TB - 1), None, ("wo0", 1, TB - 1))
    for kind, b in block_order(FFN_BLOCKS):
        short = b == FFN_BLOCKS - 1
        if kind == "down":
            add(("ffn", kind, b), *([("fy", DH - 1, TB - 1)] if short else [None, None]))
        else:
            add(("ffn", kind, b), None, ("f" + kind[0], b, 0 if short else 1))
    add("q1", None, ("q1", 1), None, ("q1", 3))
    add("k1", None, ("k1", 1), None, ("k1", 3))
    add("v1", None, ("v1", 0, TB - 1), None, ("v1", 1, TB - 1))
    add("wo1", None, ("wo1", 0, TB - 1), None, ("wo1", 1, TB - 1))
    at["moe"] = len(ends)
    for kind, b in block_order(BLOCKS):
        if kind == "down":
            add(("moe", kind, b), None, ("y", DH - 1) if b == BLOCKS - 1 else None)
        else:
            add(("moe", kind, b), None, (kind[0], b))
    return ends, at


ENDS, AT = unit_ends()
N_MOE = AT["moe"]
MOE_UNITS = len(ENDS) - N_MOE
assert MOE_UNITS % RAW == 0 and MOE_UNITS % SPLIT == 0
COUNTED = np.cumsum([key is None for key in ENDS]).tolist()
MOE_COUNTED = COUNTED[-1] - COUNTED[N_MOE - 1]


def end(name):
    n = AT[name]
    later = [v for v in list(AT.values()) + [len(ENDS)] if v > n]
    return min(later) - 1


C_IDENT, C_TRI, C_BEFORE, C_FLIP, C_IOTA = 0, P, 2 * P, 3 * P, 4 * P
C_DESC = C_IOTA + CAP
C_COLS = C_DESC + E


def constants():
    c = np.zeros((P, C_COLS), np.float32)
    i, j = np.arange(P)[:, None], np.arange(P)[None, :]
    c[:, C_IDENT:C_IDENT + P] = i == j
    c[:, C_TRI:C_TRI + P] = -(i >= j).astype(np.float32)
    c[:, C_BEFORE:C_BEFORE + P] = i < j
    c[:, C_FLIP:C_FLIP + P] = i + j == P - 1
    c[:, C_IOTA:C_IOTA + CAP] = np.arange(CAP)
    c[:, C_DESC:C_DESC + E] = E - np.arange(E)
    return c


def bucket_rows():
    dist = (-np.arange(2 * WINDOW)) % WINDOW
    exact = BUCKETS // 2
    far = np.maximum(dist, 1).astype(np.float32)
    large = exact + (np.log(far / np.float32(exact)) / np.float32(np.log(MAX_DIST / exact))
                     * np.float32(BUCKETS - exact)).astype(np.int32)
    bucket = np.where(dist < exact, dist, np.minimum(large, BUCKETS - 1))
    return (np.arange(BUCKETS)[:, None] == bucket[None, :]).astype(np.float32)


class Uses:

    def __init__(self):
        self.at, self.fills, self.frees, self.next = {}, [0] * 8, [0] * 8, 0

    def use(self, key, bank=None, counted=True):
        if bank is None:
            bank = self.next
            self.next = (bank + 1) % 8
        self.at[key] = (bank, self.fills[bank], self.frees[bank])
        self.fills[bank] += 1
        self.frees[bank] += counted


def plan():
    u = Uses()
    u.use("biases")
    u.use("bias rows")

    def transposed(name):
        for j in range(4):
            u.use((name, j))

    transposed("hT0")
    for j in range(FT // 2):
        u.use(("q", j))
    u.use("k")
    u.use("v")
    for n in range(4):
        u.use(("toeplitz", n))
    for g in range(H // GROUP + 2):
        if g < H // GROUP:
            for half in range(2):
                u.use(("s1", g, half))
                u.use(("s0", g, half))
        if 1 <= g <= H // GROUP:
            for t in range(3):
                u.use(("pT", g - 1, t))
        if g >= 2:
            u.use(("o", g - 2))
    transposed("oT0")
    for dh in range(DH):
        for tb in range(TB):
            u.use(("wo0", dh, tb))
    transposed("hT1")
    for b in range(FFN_BLOCKS):
        for c in range(2 if b < FFN_BLOCKS - 1 else 1):
            u.use(("fg", b, c), c)
            u.use(("fu", b, c), 2 + c)
    for tb in range(TB):
        for dh in range(DH):
            u.use(("fy", dh, tb), 4 + 2 * tb + dh)
    transposed("hT2")
    for j in range(FT // 2):
        u.use(("q1", j))
    for j in range(FT // 2):
        u.use(("k1", j))
    for vh in range(2):
        for tb in range(TB):
            u.use(("v1", vh, tb))
    for b in range(FT):
        for half in range(2):
            u.use(("z", b, half), (2 * b + half) % 6)
    for n in range(FT // 2):
        u.use(("so", n), 6 + n % 2)
    transposed("oT1")
    for dh in range(DH):
        for tb in range(TB):
            u.use(("wo1", dh, tb))
    transposed("hT3")
    u.use("logits")
    u.use("places")
    u.use(("first gather", 0), 7, counted=False)
    u.use(("first gather", 1), 6, counted=False)
    fills, frees = list(u.fills), list(u.frees)
    for b in range(BLOCKS):
        u.use(("g", b), b % 2)
        u.use(("u", b), 2 + b % 2)
        if b == 0:
            u.use("gates", 7)
        else:
            u.use(("hidT", b - 1), 6 + (b - 1) % 2)
    u.use(("hidT", BLOCKS - 1), 6 + (BLOCKS - 1) % 2)
    for dh in range(DH):
        u.use(("y", dh), 4 + dh)
    u.use(("gather", 0), 7, counted=False)
    u.use(("gather", 1), 6, counted=False)
    for n in range(TB * DH):
        u.use(("scatter", n), 7 - n % 2)
        b, full, free = u.at[("scatter", n)]
        u.at[("last scatter", n)] = (b, full - 1, free)
    return u.at, [b - a for a, b in zip(fills, u.fills)], [b - a for a, b in zip(frees, u.frees)]


USES, FILLS, FREES = plan()
IN_LOOP = {"g", "u", "y", "gates", "gather", "scatter", "last scatter", "hidT"}


def looped(key):
    return (key if isinstance(key, str) else key[0]) in IN_LOOP


class Steps:

    def __init__(self, engine, sem):
        self.engine, self.sem, self.n, self.i, self.each = engine, sem, 0, None, 0

    def mark(self, instruction):
        instruction.then_inc(self.sem, 1)
        self.n += 1

    def settle(self):
        self.engine.wait_ge(self.sem, self.n if self.i is None else self.i * self.each + self.n)

    def loop(self, i, each):
        self.i, self.each, self.start = i, each, self.n

    def end(self):
        assert self.n - self.start == self.each, (self.n - self.start, self.each)


def build(nc, a):
    ctx = ExitStack()
    with ctx:
        def sb(name, shape, dt=F32):
            return ctx.enter_context(nc.sbuf_tensor(name, shape, dt))

        def sem(name):
            return ctx.enter_context(nc.semaphore(name))

        raw = [sb(f"raw{n}", [P, HALF_T, HALF]) for n in range(RAW)]
        high = [sb(f"high{n}", [P, HALF_T, HALF], F32R) for n in range(SPLIT)]
        low = [sb(f"low{n}", [P, HALF_T, HALF], F32R) for n in range(SPLIT)]
        x = sb("x", [P, TB, D])
        h = sb("h", [P, TB, D])
        inT_high = sb("inT_high", [P, DT, SEQ], F32R)
        inT_low = sb("inT_low", [P, DT, SEQ], F32R)
        qT = sb("qT", [P, FT, SEQ])
        o = sb("o", [P, TB, D])
        kv_area = sb("kv_area", [P, 4096])
        work = sb("work", [P, 4608])
        hid_high = sb("hid_high", [P, 2 * HALF], F32R)
        hid_low = sb("hid_low", [P, 2 * HALF], F32R)
        consts = sb("consts", [P, C_COLS])
        ones = sb("ones", [P, P])
        minus_ones = sb("minus_ones", [P, P])
        bias_tiles = sb("bias_tiles", [(H + KV) * HD // P, P])
        biases = sb("biases", [P, (H + KV) * HD // P])
        gain_row = sb("gain_row", [P, D])
        v_bias = sb("v_bias", [1, KV * HD])
        sinks = sb("sinks", [P, H])
        minus_sinks = sb("minus_sinks", [P, H])
        k_swa = sb("k_swa", [P, SEQ])
        kT_swa = sb("kT_swa", [P, KV, SEQ])
        v_swa = sb("v_swa", [P, TB, KV * HD])
        rel = sb("rel", [BUCKETS, H])
        router = sb("router", [P, DT, E])
        sumsq = sb("sumsq", [P, TB])
        meansq = sb("meansq", [P, TB])
        root = sb("root", [P, TB])
        rstd = sb("rstd", [P, TB])
        peak = sb("peak", [P, 2, TB, GROUP])
        shift = sb("shift", [P, 2, TB, GROUP])
        sink_gap = sb("sink_gap", [P, 2, TB, GROUP])
        sink_exp = sb("sink_exp", [P, 2, TB, GROUP])
        row_sum = sb("row_sum", [P, 2, TB, GROUP])
        total = sb("total", [P, 2, TB, GROUP])
        inverse = sb("inverse", [P, 2, TB, GROUP])
        route = sb("route", [P, 12, TB, E])
        picks = sb("picks", [P, 12, TB])
        crowd = sb("crowd", [P, 8])
        posm = sb("posm", [P, TB, E])
        comb = sb("comb", [P, TB, E])
        pcol = sb("pcol", [P, TB, 1])
        ccol = sb("ccol", [P, TB, 1])
        n_items = sb("n_items", [P, 1], I32)

        ident = consts[:, C_IDENT:C_IDENT + P]
        tri = consts[:, C_TRI:C_TRI + P]
        before = consts[:, C_BEFORE:C_BEFORE + P]
        flip = consts[:, C_FLIP:C_FLIP + P]
        iota = consts[:, C_IOTA:C_IOTA + CAP]
        desc = consts[:, C_DESC:C_DESC + E]

        bias_mask = kv_area[:, :].rearrange("p (h k) -> p h k", h=H)
        toeplitz = work[:, 0:H * WINDOW].rearrange("p (h k) -> p h k", h=H)
        onehot = qT[0:BUCKETS, 0, 0:2 * WINDOW]
        hankel = o[:, :, :].rearrange("p t d -> p (t d)")
        bias_rows = work[0:H, H * WINDOW:H * WINDOW + 2 * WINDOW]
        score = [work[:, n * 1536:(n + 1) * 1536].rearrange("p (a k) -> p a k", a=GROUP) for n in range(2)]
        probT = work[:, 3072:4608]
        kT = kv_area[:, 0:2048].rearrange("p (t s) -> p t s", t=FT)
        v_sb = kv_area[:, 2048:4096].rearrange("p (t s) -> p t s", t=TB)
        soft = [work[:, n * 768:(n + 1) * 768].rearrange("p (a k) -> p a k", a=2) for n in range(2)]
        fail = [work[:, (2 + n) * 768:(3 + n) * 768].rearrange("p (a k) -> p a k", a=2) for n in range(2)]
        stick = [work[:, (4 + n) * 768:(5 + n) * 768].rearrange("p (a k) -> p a k", a=2) for n in range(2)]
        f_silu = work[:, 0:2 * HALF]
        f_prod = work[:, 2 * HALF:4 * HALF]
        routed = qT
        e_silu = [work[0:CAP, n * HALF:(n + 1) * HALF] for n in range(2)]
        e_prod = [work[0:CAP, (2 + n) * HALF:(3 + n) * HALF] for n in range(2)]
        gathered_high = inT_high[:, 0:DT * CAP // SEQ, :].rearrange("p t (c s) -> p (t c) s", s=CAP)
        gathered_low = inT_low[:, 0:DT * CAP // SEQ, :].rearrange("p t (c s) -> p (t c) s", s=CAP)
        w0 = 4 * HALF
        place = work[:, w0:w0 + TB * CAP].rearrange("p (t s) -> p t s", t=TB)
        w0 += TB * CAP
        weighted = work[:, w0:w0 + TB * CAP].rearrange("p (t s) -> p t s", t=TB)
        w0 += TB * CAP
        gates = work[0:CAP, w0:w0 + SEQ]
        y_sb = qT[0:CAP, 0:D // SEQ, :].rearrange("p t s -> p (t s)")

        bank = ctx.enter_context(nc.psum_tensor("bank", [P, 8, HALF], F32))
        bias_dram = nc.dram_tensor("bias_dram", [H, 2 * WINDOW], F32)

        raw_full = [sem(f"raw_full{n}") for n in range(RAW)]
        high_done = sem("high_done")
        low_done = sem("low_done")
        units_used = sem("units_used")
        minus_sinks_ready = sem("minus_sinks_ready")
        final_rstd = sem("final_rstd")
        psum_full = [sem(f"psum_full{n}") for n in range(8)]
        psum_free = [sem(f"psum_free{n}") for n in range(8)]
        x_loaded = [sem(f"x_loaded{tb}") for tb in range(TB)]
        consts_loaded = sem("consts_loaded")
        biases_loaded = sem("biases_loaded")
        rel_loaded = sem("rel_loaded")
        small_loaded = sem("small_loaded")
        gain_loaded = sem("gain_loaded")
        input_high_ready = sem("input_high_ready")
        f_high_ready = sem("f_high_ready")
        f_low_ready = sem("f_low_ready")
        gathered_high_ready = sem("gathered_high_ready")
        ones_set = sem("ones_set")
        rows_ready = sem("rows_ready")
        rows_stored = sem("rows_stored")
        hankel_loaded = sem("hankel_loaded")
        bias_ready = sem("bias_ready")
        sumsq_ready = sem("sumsq_ready")
        meansq_ready = sem("meansq_ready")
        root_ready = sem("root_ready")
        h_ready = sem("h_ready")
        k_swa_ready = sem("k_swa_ready")
        max_ready = sem("max_ready")
        exp_done = sem("exp_done")
        z_ready = sem("z_ready")
        clamped_ready = sem("clamped_ready")
        soft_ready = sem("soft_ready")
        fail_ready = sem("fail_ready")
        fail_masked = sem("fail_masked")
        stick_masked = sem("stick_masked")
        gap_ready = sem("gap_ready")
        gap_exp = sem("gap_exp")
        picks_ready = sem("picks_ready")
        items_ready = sem("items_ready")
        place_ready = sem("place_ready")
        gathered_ready = sem("gathered_ready")
        weighted_ready = sem("weighted_ready")
        act_steps = sem("act_steps")
        dve_steps = sem("dve_steps")
        trunk_done = sem("trunk_done")
        final_sumsq = sem("final_sumsq")
        final_meansq = sem("final_meansq")
        final_root = sem("final_root")
        result_ready = sem("result_ready")
        stored = sem("stored")

        def begin(pe, key, i=None):
            b, _, n = USES[key]
            if looped(key):
                pe.wait_ge(psum_free[b], i * FREES[b] + n)
            elif n > 0:
                pe.wait_ge(psum_free[b], n)
            return bank[:, b, :]

        def filled(ins, key):
            ins.then_inc(psum_full[USES[key][0]], 1)

        def full(eng, key, i=None):
            b, n, _ = USES[key]
            eng.wait_ge(psum_full[b], i * FILLS[b] + (n + 1) if looped(key) else n + 1)
            return bank[:, b, :]

        def freed(ins, key):
            ins.then_inc(psum_free[USES[key][0]], 1)

        def taken(eng, key, i=None):
            b, _, n = USES[key]
            eng.wait_ge(psum_free[b], i * FREES[b] + (n + 1) if looped(key) else n + 1)

        def used(eng, n, i=None):
            key = ENDS[n]
            if key is not None:
                full(eng, key, i)
            elif n < N_MOE:
                eng.wait_ge(units_used, COUNTED[n])
            else:
                eng.wait_ge(units_used, i * MOE_COUNTED + COUNTED[n])

        def through(n, i):
            return n + 1 if i is None else i * MOE_UNITS + (n + 1)

        narrow = {n: 2 * KV * HD for n in (AT["qkv0"] + 4, AT["qkv0"] + 5)}
        for kind in ("gate", "up"):
            for n in range(2):
                narrow[AT[("ffn", kind, FFN_BLOCKS - 1)] + n] = FFN - (FFN_BLOCKS - 1) * HALF

        def make_high(act, n, i=None):
            r = n % RAW
            value = 16 * (n // RAW + 1)
            act.wait_ge(raw_full[r], value if i is None else i * (16 * MOE_UNITS // RAW) + value)
            if n - SPLIT >= N_MOE:
                used(act, n - SPLIT, i)
            elif i is not None and not isinstance(i, int):
                used(act, n - SPLIT + MOE_UNITS, i - 1)
            elif n >= SPLIT:
                used(act, n - SPLIT)
            c = narrow.get(n, HALF)
            nc.scalar.copy(high[n % SPLIT][:, :, 0:c], raw[r][:, :, 0:c]).then_inc(high_done, 1)

        def make_low(dve, n, i=None):
            dve.wait_ge(high_done, through(n, i))
            c = narrow.get(n, HALF)
            nc.vector.tensor_tensor(low[n % SPLIT][:, :, 0:c], raw[n % RAW][:, :, 0:c],
                                    high[n % SPLIT][:, :, 0:c].bitcast(F32), ALU.subtract).then_inc(low_done, 1)

        def by_rows(slot):
            return slot[:, :, :].rearrange("p (t c) n -> p t (c n)", c=DH)

        block = ctx.enter_context(nc.Block())

        @block.sync
        def _(sp):
            for tb in range(TB):
                sp.dma_start(x[:, tb, :], a["x"][0, tb * P:(tb + 1) * P, :]).then_inc(x_loaded[tb], 16)

            def load(n, dst, src, i=None):
                if i is not None or n >= RAW:
                    sp.wait_ge(low_done, through(n - RAW, i))
                sp.dma_start(dst, src).then_inc(raw_full[n % RAW], 16)

            def columns(n, w, c0, c1, i=None):
                for k in range(2):
                    r0 = k * HALF_T * P
                    load(n + k, raw[(n + k) % RAW][:, :, 0:c1 - c0],
                         w[r0:r0 + HALF_T * P, c0:c1].rearrange("(t p) n -> p t n", p=P), i)

            def rows(n, w, r0, r1, i=None):
                for k in range((r1 - r0) // (2 * P)):
                    lo = r0 + 2 * k * P
                    load(n + k, by_rows(raw[(n + k) % RAW]), w[lo:lo + 2 * P, :].rearrange("(t p) n -> p t n", p=P), i)

            w = a["swa_w_qkv"][0]
            for n in range(3):
                columns(AT["qkv0"] + 2 * n, w, n * HALF, min((n + 1) * HALF, w.shape[1]))
            for dh in range(DH):
                columns(AT["wo0"] + 2 * dh, a["swa_w_o"][0], dh * HALF, (dh + 1) * HALF)
            for kind, b in block_order(FFN_BLOCKS):
                lo, hi = b * HALF, min((b + 1) * HALF, FFN)
                (rows if kind == "down" else columns)(AT[("ffn", kind, b)], a["ffn_w_" + kind][0], lo, hi)
            for n in range(6):
                columns(AT["q1"] + 2 * n, a["sb_w_qkv"][0], n * HALF, (n + 1) * HALF)
            for dh in range(DH):
                columns(AT["wo1"] + 2 * dh, a["sb_w_o"][0], dh * HALF, (dh + 1) * HALF)

            def expert_loads(e, i):
                for kind, b in block_order(BLOCKS):
                    lo, hi = b * HALF, (b + 1) * HALF
                    whole = a["moe_w_" + kind][0]
                    if kind == "down":
                        rows(AT[("moe", kind, b)], whole[bass.ds(e, 1), lo:hi, :].rearrange("o f d -> (o f) d"), 0, HALF, i)
                    else:
                        columns(AT[("moe", kind, b)], whole[bass.ds(e, 1), :, lo:hi].rearrange("o d f -> (o d) f"), 0, HALF, i)

            with sp.Fori(0, E) as i:
                expert_loads(i, i)
            sp.wait_ge(items_ready, 1)
            items = sp.value_load(n_items[0:1, 0:1], min_val=E, max_val=PASSES * E)
            with sp.If(items > E):
                with sp.Fori(E, items, E) as before_pass:
                    with sp.Fori(0, E) as e:
                        expert_loads(e, before_pass + e)

            for tb in range(TB):
                sp.wait_ge(result_ready, tb + 1)
                sp.dma_start(a["out"][0, tb * P:(tb + 1) * P, :], h[:, tb, :]).then_inc(stored, 16)
            sp.wait_ge(stored, 16 * TB)

        @block.gpsimd
        def _(pool):
            nc.gpsimd.memset(ones[:, :], 1.0).then_inc(ones_set, 1)
            nc.gpsimd.memset(minus_ones[:, :], -1.0).then_inc(ones_set, 1)
            for n in range(4):
                taken(pool, ("toeplitz", n))
            nc.gpsimd.affine_select(out=bias_mask[:, :, WINDOW:2 * WINDOW], in_=toeplitz, compare_op=ALU.is_ge,
                                    fill=MASKED, base=0, pattern=[[0, H], [-1, WINDOW]],
                                    channel_multiplier=1).then_inc(bias_ready, 1)
            nc.gpsimd.affine_select(out=bias_mask[:, :, 0:WINDOW], in_=toeplitz, compare_op=ALU.is_gt,
                                    fill=MASKED, base=0, pattern=[[0, H], [1, WINDOW]],
                                    channel_multiplier=-1).then_inc(bias_ready, 1)

            def strictly_causal(t, done):
                for half in range(2):
                    blocks = t[:, half, :].rearrange("p (b k) -> p b k", b=3)[:, 0:3:2, :]
                    ins = nc.gpsimd.affine_select(out=blocks, in_=blocks, compare_op=ALU.is_gt, fill=0.0, base=0,
                                                  pattern=[[0, 2], [1, P]], channel_multiplier=-1)
                ins.then_inc(done, 1)

            for b in range(FT + 1):
                if b < FT:
                    pool.wait_ge(fail_ready, b + 1)
                    strictly_causal(fail[b % 2], fail_masked)
                if b >= 1:
                    for half in range(2):
                        taken(pool, ("z", b - 1, half))
                    strictly_causal(stick[(b - 1) % 2], stick_masked)

        @block.scalar
        def _(act):
            def load_gain(k):
                row = [a["attn_norm"][0:1], a["ffn_norm"][0:1], a["attn_norm"][1:2], a["ffn_norm"][1:2],
                       a["final_norm"].rearrange("(o d) -> o d", o=1)][k]
                if k > 0:
                    act.wait_ge(h_ready, TB * k)
                act.dma_start(gain_row[:, :], row.to_broadcast([P, D])).then_inc(gain_loaded, 16)

            act.dma_start(consts[:, :], a["consts"]).then_inc(consts_loaded, 16)
            load_gain(0)
            act.dma_start(rel[:, :], a["rel_bias"]).then_inc(rel_loaded, 16)
            act.dma_start(onehot, a["onehot"]).then_inc(rel_loaded, 16)
            act.dma_start(bias_tiles[:, :], a["swa_b_qkv"][0, 0:(H + KV) * HD].rearrange("(t p) -> t p", p=P)).then_inc(biases_loaded, 16)
            act.dma_start(v_bias[:, :], a["swa_b_qkv"][:, (H + KV) * HD:]).then_inc(small_loaded, 16)
            act.dma_start(sinks[:, :], a["swa_sinks"].to_broadcast([P, H])).then_inc(small_loaded, 16)
            act.dma_start(router[:, :, :], a["moe_router"][0].rearrange("(t p) e -> p t e", p=P)).then_inc(small_loaded, 16)

            steps = Steps(act, act_steps)
            highs = [0]

            def split_to(n):
                while highs[0] <= n:
                    make_high(act, highs[0])
                    highs[0] += 1

            def norm(k, x_from):
                nc.scalar.preload_act_table(ACT.Sqrt)
                for tb in range(TB):
                    if k == 0:
                        act.wait_ge(x_loaded[tb], 16)
                    for key in x_from:
                        if key[-1] == tb:
                            taken(act, key)
                    nc.scalar.activation(h[:, tb, :], x[:, tb, :], ACT.Square,
                                         accum_out=sumsq[:, tb:tb + 1]).then_inc(sumsq_ready, 1)
                act.wait_ge(meansq_ready, k + 1)
                nc.scalar.activation(root[:, :], meansq[:, :], ACT.Sqrt).then_inc(root_ready, 1)

            def input_high(name):
                for j in range(4):
                    b = full(act, (name, j))
                    nc.scalar.copy(inT_high[:, 2 * j:2 * j + 2, :].rearrange("p t s -> p (t s)"), b).then_inc(input_high_ready, 1)

            norm(0, [])
            b = full(act, "bias rows")
            freed(nc.scalar.copy(bias_rows, b[0:H, 0:2 * WINDOW]), "bias rows")
            taken(act, "bias rows")
            act.dma_start(bias_dram.ap(), bias_rows).then_inc(rows_stored, 16)
            split_to(SPLIT - 1)
            input_high("hT0")
            act.wait_ge(rows_stored, 16)
            act.dma_start(hankel.rearrange("p (h k) -> p h k", h=H),
                          bass.AP(bias_dram, 1, [[1, P], [2 * WINDOW, H], [1, WINDOW]])).then_inc(hankel_loaded, 16)
            load_gain(1)
            split_to(end("qkv0") + 2)
            b = full(act, "v")
            freed(nc.scalar.copy(v_swa[:, :, :].rearrange("p t s -> p (t s)"), b[:, 0:TB * KV * HD]), "v")
            split_to(end("qkv0") + SPLIT)
            for n in range(4):
                b = full(act, ("toeplitz", n))
                freed(nc.scalar.copy(work[:, n * HALF:(n + 1) * HALF], b), ("toeplitz", n))

            for g in range(H // GROUP + 1):
                if g < H // GROUP:
                    s, m = score[g % 2], g % 2
                    act.wait_ge(max_ready, g + 1)
                    for n in range(GROUP):
                        for tb, c0, c1 in ((1, 0, 2 * P), (0, 2 * P, 3 * P)):
                            nc.scalar.activation(s[:, n, c0:c1], s[:, n, c0:c1], ACT.Exp,
                                                 bias=shift[:, m, tb, n:n + 1],
                                                 accum_out=row_sum[:, m, tb, n:n + 1])
                    nc.scalar.activation(sink_exp[:, m, :, :], sink_gap[:, m, :, :], ACT.Exp).then_inc(exp_done, 1)
                if g >= 1:
                    if g >= 2:
                        full(act, ("o", g - 2))
                    for t in range(3):
                        b = full(act, ("pT", g - 1, t))
                        freed(nc.scalar.copy(probT[:, t * HALF:(t + 1) * HALF], b), ("pT", g - 1, t))
            input_high("oT0")
            split_to(end("wo0") + SPLIT - 1)
            norm(1, [("wo0", dh, tb) for dh in range(DH) for tb in range(TB)])
            split_to(end("wo0") + SPLIT)
            input_high("hT1")
            load_gain(2)

            def ffn_high(b):
                cols = 2 * HALF if b < FFN_BLOCKS - 1 else HALF
                for c in range(cols // HALF):
                    taken(act, ("fu", b, c))
                if b >= 1:
                    used(act, end(("ffn", "down", b - 1)))
                nc.scalar.copy(hid_high[:, 0:cols], f_prod[:, 0:cols]).then_inc(f_high_ready, 1)

            for kind, b in block_order(FFN_BLOCKS):
                split_to(end(("ffn", kind, b)) + SPLIT - 1)
                if kind == "gate":
                    for c in range(2 if b < FFN_BLOCKS - 1 else 1):
                        p = full(act, ("fg", b, c))
                        freed(nc.scalar.activation(f_silu[:, c * HALF:(c + 1) * HALF], p, ACT.Silu), ("fg", b, c))
                elif kind == "up" and b == 0:
                    ffn_high(0)
                elif kind == "down" and b < FFN_BLOCKS - 1:
                    ffn_high(b + 1)
            norm(2, [("fy", dh, tb) for tb in range(TB) for dh in range(DH)])
            split_to(end(("ffn", "down", FFN_BLOCKS - 1)) + SPLIT)
            input_high("hT2")
            load_gain(3)
            split_to(end("q1") + SPLIT - 1)
            for j in range(FT // 2):
                split_to(AT["k1"] + j // 2 * 2 + SPLIT)
                b = full(act, ("k1", j))
                freed(nc.scalar.copy(kT[:, 2 * j:2 * j + 2, :].rearrange("p t s -> p (t s)"), b), ("k1", j))
            split_to(end("v1") + SPLIT - 1)

            nc.scalar.preload_act_table_set("natural_log_exp_and_others")
            for b in range(FT + 1):
                if b < FT:
                    act.wait_ge(clamped_ready, b + 1)
                    steps.mark(nc.scalar.activation(soft[b % 2], soft[b % 2], ACT.Exp))
                    steps.settle()
                    nc.scalar.activation(soft[b % 2], soft[b % 2], ACT.Ln, bias=1.0).then_inc(soft_ready, 1)
                if b == 1:
                    split_to(end("v1") + SPLIT)
                if b >= 1:
                    c = b - 1
                    if c >= 2 and c % 2 == 0:
                        full(act, ("so", c // 2 - 1))
                    for half in range(2):
                        p = full(act, ("z", c, half))
                        freed(nc.scalar.activation(stick[c % 2][:, half, :], p[:, 0:3 * P], ACT.Exp), ("z", c, half))
            input_high("oT1")
            split_to(end("wo1") + SPLIT - 1)
            norm(3, [("wo1", dh, tb) for dh in range(DH) for tb in range(TB)])
            for j in (1, 3):
                b = full(act, ("hT3", j))
                freed(nc.scalar.copy(routed[:, 2 * j:2 * j + 2, :].rearrange("p t s -> p (t s)"), b), ("hT3", j))
            load_gain(4)
            used(act, N_MOE - 1)
            act.wait_ge(gap_ready, 1)
            nc.scalar.activation(picks[:, 5, :], picks[:, 4, :], ACT.Exp).then_inc(gap_exp, 1)

            def gathered_part(name, q, i=None):
                b = full(act, (name, q), i)
                nc.scalar.copy(gathered_high[:, 4 * q:4 * q + 4, :],
                               b.rearrange("p (t s) -> p t s", t=4)).then_inc(gathered_high_ready, 1)

            def item(i, last):
                def hidden_high(b):
                    p = full(act, ("hidT", b), i)
                    nc.scalar.copy(hid_high[:, 0:HALF], p).then_inc(input_high_ready, 1)

                done = SPLIT - 1
                for kind, b in block_order(BLOCKS):
                    n = end(("moe", kind, b)) - N_MOE
                    while done < min(n + SPLIT, MOE_UNITS if last else n + SPLIT):
                        make_high(act, N_MOE + done, i)
                        done += 1
                    if kind == "gate":
                        p = full(act, ("g", b), i)
                        freed(nc.scalar.activation(e_silu[b % 2], p[0:CAP, :], ACT.Silu), ("g", b))
                        if b >= 1:
                            hidden_high(b - 1)
                    elif kind == "up" and b == 0:
                        p = full(act, "gates", i)
                        freed(nc.scalar.copy(gates, p[0:CAP, 0:SEQ]), "gates")
                    elif kind == "down" and b == BLOCKS - 2:
                        hidden_high(BLOCKS - 1)
                        if not last:
                            for q in range(2):
                                gathered_part("gather", q, i)
                for dh in range(DH):
                    p = full(act, ("y", dh), i)
                    freed(nc.scalar.copy(y_sb[:, dh * HALF:(dh + 1) * HALF], p[0:CAP, :]), ("y", dh))

            for q in range(2):
                gathered_part("first gather", q)
            act.wait_ge(items_ready, 1)
            items = act.value_load(n_items[0:1, 0:1], min_val=E, max_val=PASSES * E)
            with act.Fori(0, items - 1) as i:
                item(i, False)
            item(items - 1, True)

            nc.scalar.preload_act_table(ACT.Sqrt)
            act.wait_ge(trunk_done, 1)
            for tb in range(TB):
                nc.scalar.activation(h[:, tb, :], x[:, tb, :], ACT.Square,
                                     accum_out=sumsq[:, tb:tb + 1]).then_inc(final_sumsq, 1)
            act.wait_ge(final_meansq, 1)
            nc.scalar.activation(root[:, :], meansq[:, :], ACT.Sqrt).then_inc(final_root, 1)

        @block.vector
        def _(dve):
            V = nc.vector
            steps = Steps(dve, dve_steps)

            lows = [0]

            def split_to(n):
                while lows[0] <= n:
                    make_low(dve, lows[0])
                    lows[0] += 1

            b = full(dve, "biases")
            freed(V.tensor_copy(biases[:, :], b[:, 0:(H + KV) * HD // P]), "biases")
            dve.wait_ge(small_loaded, 48)
            V.tensor_scalar(minus_sinks[:, :].rearrange("p (g f j) -> p g f j", g=H // GROUP, f=2),
                            sinks[:, :].rearrange("p (g j f) -> p g f j", g=H // GROUP, f=2),
                            -1.0, None, ALU.mult).then_inc(minus_sinks_ready, 1)
            taken(dve, "biases")

            def norm(k):
                dve.wait_ge(sumsq_ready, TB * (k + 1))
                V.tensor_scalar(meansq[:, :], sumsq[:, :], 1.0 / D, EPS, ALU.mult, ALU.add).then_inc(meansq_ready, 1)
                dve.wait_ge(root_ready, k + 1)
                steps.mark(V.reciprocal(rstd[:, :], root[:, :]))
                steps.settle()
                dve.wait_ge(gain_loaded, 16 * (k + 1))
                for tb in range(TB):
                    V.scalar_tensor_tensor(h[:, tb, :], x[:, tb, :], rstd[:, tb:tb + 1], gain_row[:, :],
                                           ALU.mult, ALU.mult).then_inc(h_ready, 1)

            inputs = [0]

            def input_low(name):
                for j in range(4):
                    inputs[0] += 1
                    dve.wait_ge(input_high_ready, inputs[0])
                    part = slice(2 * j, 2 * j + 2)
                    b = bank[:, USES[(name, j)][0], :].rearrange("p (t s) -> p t s", t=2)
                    freed(V.tensor_tensor(inT_low[:, part, :], b, inT_high[:, part, :].bitcast(F32), ALU.subtract), (name, j))

            def add_to_x(key, tb, dh, i=None):
                b = full(dve, key, i)
                part = x[:, tb, dh * HALF:(dh + 1) * HALF]
                ins = V.tensor_tensor(part, part, b, ALU.add)
                freed(ins, key)
                return ins

            norm(0)
            split_to(SPLIT - 1)
            input_low("hT0")

            for j in range(FT // 2):
                split_to(AT["qkv0"] + j // 2 * 2 + SPLIT)
                b = full(dve, ("q", j))
                for s in range(2):
                    t = 2 * j + s
                    ins = V.tensor_scalar(qT[:, t, :], b[:, s * SEQ:(s + 1) * SEQ], biases[:, t:t + 1], SCALE,
                                          ALU.add, ALU.mult)
                freed(ins, ("q", j))
            split_to(end("qkv0") + 2)
            b = full(dve, "k")
            freed(V.tensor_scalar(k_swa[:, :], b[:, 0:SEQ], biases[:, FT:FT + 1], None, ALU.add), "k")
            taken(dve, "k")
            for kv in range(KV):
                for half in range(2):
                    ins = V.tensor_copy(kT_swa[half * HD:(half + 1) * HD, kv, :], k_swa[kv * HD:(kv + 1) * HD, :])
            ins.then_inc(k_swa_ready, 1)
            split_to(end("qkv0") + SPLIT)

            dve.wait_ge(bias_ready, 2)
            dve.wait_ge(minus_sinks_ready, 1)
            for g in range(H // GROUP + 2):
                if g < H // GROUP:
                    s, m = score[g % 2], g % 2
                    for half in range(2):
                        first = GROUP * g + half
                        for kind, c0, c1 in (("s1", 0, 2 * P), ("s0", 2 * P, 3 * P)):
                            b = full(dve, (kind, g, half))
                            n = c1 - c0
                            freed(V.tensor_tensor(s[:, 2 * half:2 * half + 2, c0:c1],
                                                  b[:, 0:2 * n].rearrange("p (j k) -> p j k", j=2),
                                                  bias_mask[:, first:first + 3:2, 2 * P - n:2 * P], ALU.add),
                                  (kind, g, half))
                    for half in range(2):
                        for kind in ("s1", "s0"):
                            taken(dve, (kind, g, half))
                    V.tensor_reduce(peak[:, m, 1, :], s[:, :, 0:2 * P], axis=AX.X, op=ALU.max)
                    steps.mark(V.tensor_reduce(peak[:, m, 0, :], s[:, :, 2 * P:3 * P], axis=AX.X, op=ALU.max))
                    steps.settle()
                    ms = minus_sinks[:, GROUP * g:GROUP * (g + 1)].unsqueeze(1).to_broadcast([P, TB, GROUP])
                    steps.mark(V.scalar_tensor_tensor(shift[:, m, :, :], peak[:, m, :, :], -1.0, ms, ALU.mult, ALU.min))
                    steps.settle()
                    V.tensor_tensor(sink_gap[:, m, :, :], shift[:, m, :, :], ms, ALU.subtract).then_inc(max_ready, 1)
                if 1 <= g <= H // GROUP:
                    m = (g - 1) % 2
                    dve.wait_ge(exp_done, g)
                    steps.mark(V.tensor_tensor(total[:, m, :, :], row_sum[:, m, :, :], sink_exp[:, m, :, :], ALU.add))
                    steps.settle()
                    steps.mark(V.reciprocal(inverse[:, m, :, :], total[:, m, :, :]))
                if g >= 2:
                    m = g % 2
                    b = full(dve, ("o", g - 2))
                    steps.settle()
                    for tb in range(TB):
                        inv = inverse[:, m, tb, :].rearrange("p (f j) -> p f j", f=2).unsqueeze(3).to_broadcast([P, 2, 2, HD])
                        w = GROUP * HD
                        ins = V.tensor_tensor(
                            o[:, tb, (g - 2) * w:(g - 1) * w].rearrange("p (j f d) -> p f j d", f=2, d=HD),
                            b[:, tb * w:(tb + 1) * w].rearrange("p (f j d) -> p f j d", f=2, d=HD), inv, ALU.mult)
                    freed(ins, ("o", g - 2))
            input_low("oT0")
            for dh in range(DH):
                split_to(AT["wo0"] + 2 * dh + SPLIT)
                for tb in range(TB):
                    add_to_x(("wo0", dh, tb), tb, dh)
            norm(1)
            split_to(end("wo0") + SPLIT)
            input_low("hT1")

            def ffn_low(b):
                cols = 2 * HALF if b < FFN_BLOCKS - 1 else HALF
                dve.wait_ge(f_high_ready, b + 1)
                V.tensor_tensor(hid_low[:, 0:cols], f_prod[:, 0:cols], hid_high[:, 0:cols].bitcast(F32),
                                ALU.subtract).then_inc(f_low_ready, 1)

            for kind, b in block_order(FFN_BLOCKS):
                split_to(end(("ffn", kind, b)) + SPLIT - 1)
                if kind == "up":
                    for c in range(2 if b < FFN_BLOCKS - 1 else 1):
                        p = full(dve, ("fu", b, c))
                        taken(dve, ("fg", b, c))
                        dve.wait_ge(f_low_ready, b) if b else None
                        cols = slice(c * HALF, (c + 1) * HALF)
                        freed(V.tensor_tensor(f_prod[:, cols], f_silu[:, cols], p, ALU.mult), ("fu", b, c))
                    if b == 0:
                        ffn_low(0)
                elif kind == "down" and b < FFN_BLOCKS - 1:
                    ffn_low(b + 1)
            for tb in range(TB):
                for dh in range(DH):
                    add_to_x(("fy", dh, tb), tb, dh)
            norm(2)
            split_to(end(("ffn", "down", FFN_BLOCKS - 1)) + SPLIT)
            input_low("hT2")

            for j in range(FT // 2):
                split_to(AT["q1"] + j // 2 * 2 + SPLIT)
                b = full(dve, ("q1", j))
                freed(V.tensor_scalar(qT[:, 2 * j:2 * j + 2, :].rearrange("p t s -> p (t s)"), b, SCALE, None,
                                      ALU.mult), ("q1", j))
            split_to(end("k1") + SPLIT - 1)
            for vh in range(2):
                split_to(AT["v1"] + 2 * vh + SPLIT)
                for tb in range(TB):
                    b = full(dve, ("v1", vh, tb))
                    freed(V.tensor_copy(v_sb[:, tb, vh * HALF:(vh + 1) * HALF], b), ("v1", vh, tb))
            for b in range(FT + 3):
                if b == 2:
                    split_to(end("v1") + SPLIT)
                if b < FT:
                    lo = 2 * b % 6
                    dve.wait_ge(z_ready, b + 1)
                    V.tensor_scalar(soft[b % 2], bank[:, lo:lo + 2, 0:3 * P], SOFT_TOP, None, ALU.min).then_inc(clamped_ready, 1)
                if 1 <= b <= FT:
                    c = b - 1
                    lo = 2 * c % 6
                    dve.wait_ge(soft_ready, b)
                    if c >= 2:
                        for half in range(2):
                            full(dve, ("z", c - 2, half))
                    V.tensor_tensor(fail[c % 2], bank[:, lo:lo + 2, 0:3 * P], soft[c % 2], ALU.max).then_inc(fail_ready, 1)
                if b >= 4 and b % 2 == 0:
                    n, w = b // 2 - 2, GROUP * HD
                    p = full(dve, ("so", n))
                    freed(V.tensor_copy(o[:, :, n * w:(n + 1) * w], p.rearrange("p (t c) -> p t c", t=TB)), ("so", n))
            input_low("oT1")
            for dh in range(DH):
                split_to(AT["wo1"] + 2 * dh + SPLIT)
                for tb in range(TB):
                    add_to_x(("wo1", dh, tb), tb, dh)
            norm(3)
            for j in (0, 2):
                b = full(dve, ("hT3", j))
                freed(V.tensor_copy(routed[:, 2 * j:2 * j + 2, :].rearrange("p t s -> p (t s)"), b), ("hT3", j))

            def link(ins):
                steps.mark(ins)
                steps.settle()

            def wide(v):
                return v.unsqueeze(2).to_broadcast([P, TB, E])

            dsc = desc.unsqueeze(1).to_broadcast([P, TB, E])
            R = [route[:, n, :, :] for n in range(12)]
            K = [picks[:, n, :] for n in range(12)]
            logits = R[0]
            b = full(dve, "logits")
            freed(V.tensor_copy(logits, b[:, 0:TB * E].rearrange("p (t e) -> p t e", t=TB)), "logits")
            taken(dve, "logits")

            def largest(values, top, first, spare):
                link(V.tensor_reduce(top, values, axis=AX.X, op=ALU.max))
                link(V.tensor_tensor(spare[0], values, wide(top), ALU.is_equal))
                link(V.tensor_tensor(spare[0], spare[0], dsc, ALU.mult))
                link(V.tensor_reduce(spare[1], spare[0], axis=AX.X, op=ALU.max))
                link(V.tensor_tensor(first, spare[0], wide(spare[1]), ALU.is_equal))

            largest(logits, K[0], R[1], (R[2], K[1]))
            link(V.scalar_tensor_tensor(R[3], R[1], -3e38, logits, ALU.mult, ALU.add))
            largest(R[3], K[2], R[4], (R[5], K[3]))
            V.tensor_tensor(K[4], K[2], K[0], ALU.subtract).then_inc(gap_ready, 1)
            V.tensor_tensor(R[6], R[1], R[4], ALU.add).then_inc(picks_ready, 1)
            dve.wait_ge(gap_exp, 1)
            link(V.tensor_scalar(K[6], K[5], 1.0, None, ALU.add))
            link(V.reciprocal(K[7], K[6]))
            link(V.tensor_tensor(K[8], K[5], K[7], ALU.mult))
            link(V.tensor_tensor(R[7], R[1], wide(K[7]), ALU.mult))
            link(V.tensor_tensor(R[8], R[4], wide(K[8]), ALU.mult))
            link(V.tensor_tensor(comb[:, :, :], R[7], R[8], ALU.add))
            b = full(dve, "places")
            link(V.scalar_tensor_tensor(R[9], b[:, 0:TB * E].rearrange("p (t e) -> p t e", t=TB), 1.0, R[6],
                                        ALU.add, ALU.mult))
            link(V.tensor_scalar(posm[:, :, :], R[9], -1.0, None, ALU.add))
            ins = V.tensor_reduce(crowd[:, 0:1], b[:, TB * E:(TB + 1) * E], axis=AX.X, op=ALU.max)
            freed(ins, "places")
            taken(dve, "places")
            for n in range(1, PASSES):
                V.tensor_scalar(crowd[:, n:n + 1], crowd[:, 0:1], float(n * CAP), float(E), ALU.is_gt, ALU.mult)
            link(V.memset(crowd[:, PASSES:PASSES + 1], float(E)))
            link(V.tensor_reduce(crowd[:, PASSES + 1:PASSES + 2], crowd[:, 1:PASSES + 1], axis=AX.X, op=ALU.add))
            V.tensor_copy(n_items[:, :], crowd[:, PASSES + 1:PASSES + 2]).then_inc(items_ready, 1)

            def choose(e):
                steps.mark(V.tensor_copy(pcol[:, :, :], posm[:, :, e]))
                steps.mark(V.tensor_copy(ccol[:, :, :], comb[:, :, e]))
                steps.settle()
                for tb in range(TB):
                    ins = V.tensor_scalar(place[:, tb, :], iota, pcol[:, tb, :], None, ALU.is_equal)
                ins.then_inc(place_ready, 1)

            def gathered_part(name, q, value):
                dve.wait_ge(gathered_high_ready, value)
                part = slice(4 * q, 4 * q + 4)
                b = bank[:, USES[(name, q)][0], :].rearrange("p (t s) -> p t s", t=4)
                V.tensor_tensor(gathered_low[:, part, :], b, gathered_high[:, part, :].bitcast(F32),
                                ALU.subtract).then_inc(gathered_ready, 1)

            def item(i, last):
                def hidden_low(b):
                    dve.wait_ge(input_high_ready, i * BLOCKS + (inputs[0] + b + 1))
                    freed(V.tensor_tensor(hid_low[:, 0:HALF], bank[:, USES[("hidT", b)][0], :],
                                          hid_high[:, 0:HALF].bitcast(F32), ALU.subtract), ("hidT", b))

                for tb in range(TB):
                    ins = V.tensor_scalar(weighted[:, tb, :], iota, pcol[:, tb, :], ccol[:, tb, :],
                                          ALU.is_equal, ALU.mult)
                ins.then_inc(weighted_ready, 1)
                done = SPLIT - 1
                for kind, b in block_order(BLOCKS):
                    n = end(("moe", kind, b)) - N_MOE
                    while done < min(n + SPLIT, MOE_UNITS if last else n + SPLIT):
                        make_low(dve, N_MOE + done, i)
                        done += 1
                    if kind == "gate" and b >= 1:
                        hidden_low(b - 1)
                    elif kind == "up":
                        p = full(dve, ("u", b), i)
                        taken(dve, ("g", b), i)
                        freed(V.tensor_tensor(e_prod[b % 2], e_silu[b % 2], p[0:CAP, :], ALU.mult), ("u", b))
                        if b == 0 and not last:
                            dve.wait_ge(weighted_ready, i + 1)
                            here = posm[:, :, bass.ds(i & (E - 1), 1)]
                            steps.mark(V.tensor_scalar(here, here, -float(CAP), None, ALU.add))
                            choose(bass.ds((i + 1) & (E - 1), 1))
                    elif kind == "down" and b == BLOCKS - 2:
                        hidden_low(BLOCKS - 1)
                        if not last:
                            for q in range(2):
                                gathered_part("gather", q, i * 2 + (q + 3))
                for n in range(TB * DH):
                    add_to_x(("last scatter" if last else "scatter", n), n // DH, n % DH, i)

            choose(slice(0, 1))
            for q in range(2):
                gathered_part("first gather", q, q + 1)
            dve.wait_ge(items_ready, 1)
            items = dve.value_load(n_items[0:1, 0:1], min_val=E, max_val=PASSES * E)
            with dve.Fori(0, items - 1) as i:
                steps.loop(i, 3)
                item(i, False)
                steps.end()
            item(items - 1, True)

            V.memset(crowd[:, 0:1], 0.0).then_inc(trunk_done, 1)
            dve.wait_ge(final_sumsq, TB)
            V.tensor_scalar(meansq[:, :], sumsq[:, :], 1.0 / D, EPS, ALU.mult, ALU.add).then_inc(final_meansq, 1)
            dve.wait_ge(final_root, 1)
            dve.wait_ge(gain_loaded, 16 * 5)
            V.reciprocal(rstd[:, :], root[:, :]).then_inc(final_rstd, 1)
            dve.wait_ge(final_rstd, 1)
            for tb in range(TB):
                V.scalar_tensor_tensor(h[:, tb, :], x[:, tb, :], rstd[:, tb:tb + 1], gain_row[:, :],
                                       ALU.mult, ALU.mult).then_inc(result_ready, 1)

        @block.tensor
        def _(pe):
            def mm(out, lhsT, rhs, start, stop, **kw):
                return nc.tensor.matmul(out, lhsT, rhs, start=start, stop=stop, **kw)

            def unit(n, i=None):
                pe.wait_ge(low_done, through(n, i))
                return high[n % SPLIT], low[n % SPLIT]

            def used_up(ins, n):
                if ENDS[n] is None:
                    ins.then_inc(units_used, 1)

            def product(out, left, right, start, stop, **kw):
                mm(out, left[0], right[0], start, False, **kw)
                mm(out, left[0], right[1], False, False, **kw)
                return mm(out, left[1], right[0], False, stop, **kw)

            def inputs(t, cols):
                return inT_high[:, t, cols], inT_low[:, t, cols]

            pe.wait_ge(biases_loaded, 16)
            pe.wait_ge(consts_loaded, 16)
            b = begin(pe, "biases")
            n = (H + KV) * HD // P
            filled(nc.tensor.transpose(b[:, 0:n], bias_tiles[:, :], ident[0:n, 0:n]), "biases")
            pe.wait_ge(rel_loaded, 32)
            b = begin(pe, "bias rows")
            filled(mm(b[0:H, 0:2 * WINDOW], rel[:, :], onehot, True, True), "bias rows")

            def transposed(src, name, ready=None):
                for tb in range(TB):
                    if ready is not None:
                        ready(tb)
                    for j in range(4):
                        b = begin(pe, (name, j)) if tb == 0 else bank[:, USES[(name, j)][0], :]
                        for s in range(2):
                            t = 2 * j + s
                            ins = nc.tensor.transpose(b[:, s * SEQ + tb * P:s * SEQ + (tb + 1) * P],
                                                      src[:, tb, t * P:(t + 1) * P], ident)
                        if tb == TB - 1:
                            filled(ins, (name, j))

            def transposed_h(k):
                transposed(h, f"hT{k}", lambda tb: pe.wait_ge(h_ready, TB * k + tb + 1))
                for j in range(4):
                    taken(pe, (f"hT{k}", j))

            def transposed_o(k, last):
                for key in last:
                    taken(pe, key)
                transposed(o, f"oT{k}")
                for j in range(4):
                    taken(pe, (f"oT{k}", j))

            every = slice(0, SEQ)

            def tokens(tb):
                return slice(tb * P, (tb + 1) * P)

            def by_tokens(name, n0):
                for dh in range(DH):
                    for k in range(2):
                        n = n0 + 2 * dh + k
                        w = unit(n)
                        for tb in range(TB):
                            key = (name, dh, tb)
                            b = begin(pe, key) if k == 0 else bank[:, USES[key][0], :]
                            for t in range(HALF_T):
                                ins = product(b, inputs(HALF_T * k + t, tokens(tb)), (w[0][:, t, :], w[1][:, t, :]),
                                              k == 0 and t == 0, k == 1 and t == HALF_T - 1)
                            if k == 1:
                                filled(ins, key)
                        used_up(ins, n)

            def by_features(keys, n0):
                for k in range(2):
                    w = unit(n0 + k)
                    for j, key in enumerate(keys):
                        b = begin(pe, key) if k == 0 else bank[:, USES[key][0], :]
                        for s in range(2):
                            for t in range(HALF_T):
                                cols = slice((2 * j + s) * P, (2 * j + s + 1) * P)
                                ins = product(b[:, s * SEQ:(s + 1) * SEQ], (w[0][:, t, cols], w[1][:, t, cols]),
                                              inputs(HALF_T * k + t, every), k == 0 and s == 0 and t == 0,
                                              k == 1 and t == HALF_T - 1, skip_group_check=True)
                        if k == 1:
                            filled(ins, key)
                    used_up(ins, n0 + k)

            transposed_h(0)
            for n in range(2):
                by_features([("q", 2 * n), ("q", 2 * n + 1)], AT["qkv0"] + 2 * n)
            pe.wait_ge(small_loaded, 48)
            pe.wait_ge(ones_set, 2)
            n0 = AT["qkv0"] + 4
            for k in range(2):
                w = unit(n0 + k)
                b = begin(pe, "k") if k == 0 else bank[:, USES["k"][0], :]
                for t in range(HALF_T):
                    ins = product(b[:, 0:SEQ], (w[0][:, t, 0:P], w[1][:, t, 0:P]), inputs(HALF_T * k + t, every),
                                  k == 0 and t == 0, k == 1 and t == HALF_T - 1)
                if k == 1:
                    filled(ins, "k")
                b = begin(pe, "v") if k == 0 else bank[:, USES["v"][0], :]
                for tb in range(TB):
                    out = b[:, tb * P:(tb + 1) * P]
                    if k == 0:
                        mm(out, ones[0:1, :], v_bias[:, :], tb == 0, False, skip_group_check=True)
                    for t in range(HALF_T):
                        ins = product(out, inputs(HALF_T * k + t, tokens(tb)), (w[0][:, t, P:2 * P], w[1][:, t, P:2 * P]),
                                      False, k == 1 and t == HALF_T - 1, skip_group_check=True)
                if k == 1:
                    filled(ins, "v")
                used_up(ins, n0 + k)
            pe.wait_ge(hankel_loaded, 16)
            for n in range(4):
                filled(mm(begin(pe, ("toeplitz", n)), flip, hankel[:, n * HALF:(n + 1) * HALF], True, True), ("toeplitz", n))

            def swa_scores(g):
                kv = g * GROUP // (H // KV)
                taken(pe, ("q", g))
                for half in range(2):
                    p0 = half * HD
                    for kind, tb, n in (("s1", 1, 2 * P), ("s0", 0, P)):
                        b = begin(pe, (kind, g, half))
                        for j in range(2):
                            ins = mm(b[:, j * n:(j + 1) * n], qT[p0:p0 + HD, 2 * g + j, tb * P:(tb + 1) * P],
                                     kT_swa[p0:p0 + HD, kv, 0:n], True, True)
                        filled(ins, (kind, g, half))

            def swa_transpose(g):
                s = score[g % 2].rearrange("p a k -> p (a k)")
                pe.wait_ge(exp_done, g + 1)
                for t in range(3):
                    b = begin(pe, ("pT", g, t))
                    for c in range(4):
                        ins = nc.tensor.transpose(b[:, c * P:(c + 1) * P], s[:, (4 * t + c) * P:(4 * t + c + 1) * P], ident)
                    filled(ins, ("pT", g, t))

            def swa_values(g):
                kv = g * GROUP // (H // KV)
                for t in range(3):
                    taken(pe, ("pT", g, t))
                b = begin(pe, ("o", g))
                for tb, parts in ((0, ((2, 0),)), (1, ((0, 0), (1, 1)))):
                    for n in range(GROUP):
                        out = b[:, (tb * GROUP + n) * HD:(tb * GROUP + n + 1) * HD]
                        for c, kb in parts:
                            ins = mm(out, probT[:, (3 * n + c) * P:(3 * n + c + 1) * P],
                                     v_swa[:, kb, kv * HD:(kv + 1) * HD], c == parts[0][0], c == parts[-1][0])
                filled(ins, ("o", g))

            pe.wait_ge(k_swa_ready, 1)
            taken(pe, "v")
            for g in range(H // GROUP + 2):
                if g < H // GROUP:
                    swa_scores(g)
                if 1 <= g <= H // GROUP:
                    swa_transpose(g - 1)
                if g >= 2:
                    swa_values(g - 2)
            transposed_o(0, [("o", g) for g in range(H // GROUP)])
            by_tokens("wo0", AT["wo0"])

            transposed_h(1)

            def ffn_down(b):
                n0 = AT[("ffn", "down", b)]
                pe.wait_ge(f_low_ready, b + 1)
                for k in range(end(("ffn", "down", b)) - n0 + 1):
                    w = unit(n0 + k)
                    wh, wl = by_rows(w[0]), by_rows(w[1])
                    for s in range(2):
                        for tb in range(TB):
                            for dh in range(DH):
                                key = ("fy", dh, tb)
                                first = b == 0 and k == 0 and s == 0
                                last = b == FFN_BLOCKS - 1 and s == 1
                                out = begin(pe, key) if first else bank[:, USES[key][0], :]
                                c = (2 * k + s) * SEQ + tb * P
                                cols = slice(dh * HALF, (dh + 1) * HALF)
                                ins = product(out, (hid_high[:, c:c + P], hid_low[:, c:c + P]),
                                              (wh[:, s, cols], wl[:, s, cols]), first, last)
                                if last:
                                    filled(ins, key)
                    used_up(ins, n0 + k)

            for kind, b in block_order(FFN_BLOCKS):
                if kind == "down":
                    ffn_down(b)
                else:
                    by_features([("f" + kind[0], b, c) for c in range(2 if b < FFN_BLOCKS - 1 else 1)],
                                AT[("ffn", kind, b)])

            transposed_h(2)
            for name in ("q1", "k1"):
                for n in range(2):
                    by_features([(name, 2 * n), (name, 2 * n + 1)], AT[name] + 2 * n)
            by_tokens("v1", AT["v1"])

            def sb_scores(n):
                taken(pe, ("q1", n // 2))
                taken(pe, ("k1", n // 2))
                for half in range(2):
                    p0 = half * HD
                    b = begin(pe, ("z", n, half))
                    mm(b[:, 0:SEQ], kT[p0:p0 + HD, n, 0:P], qT[p0:p0 + HD, n, :], True, False, skip_group_check=True)
                    ins = mm(b[:, SEQ:SEQ + P], kT[p0:p0 + HD, n, P:SEQ], qT[p0:p0 + HD, n, P:SEQ], False, False,
                             skip_group_check=True)
                ins.then_inc(z_ready, 1)

            def sb_sums(n):
                pe.wait_ge(fail_masked, n + 1)
                for half in range(2):
                    b = bank[:, USES[("z", n, half)][0], :]
                    f = fail[n % 2][:, half, :]
                    mm(b[:, 0:SEQ], tri, f[:, 0:SEQ], False, False, skip_group_check=True)
                    mm(b[:, P:SEQ], minus_ones[:, :], f[:, SEQ:SEQ + P], False, False, skip_group_check=True)
                    ins = mm(b[:, SEQ:SEQ + P], tri, f[:, SEQ:SEQ + P], False, True, skip_group_check=True)
                    filled(ins, ("z", n, half))

            def sb_values(n):
                if n == 0:
                    for vh in range(2):
                        for tb in range(TB):
                            taken(pe, ("v1", vh, tb))
                pe.wait_ge(stick_masked, n + 1)
                key = ("so", n // 2)
                b = begin(pe, key) if n % 2 == 0 else bank[:, USES[key][0], :]
                for half in range(2):
                    head = 2 * n + half
                    s = stick[n % 2][:, half, :]
                    vc = slice(head * HD, (head + 1) * HD)
                    for tb, parts in ((0, ((0, 0),)), (1, ((P, 0), (SEQ, 1)))):
                        c0 = tb * GROUP * HD + head % GROUP * HD
                        for m, (c, kb) in enumerate(parts):
                            ins = mm(b[:, c0:c0 + HD], s[:, c:c + P], v_sb[:, kb, vc], m == 0, m == len(parts) - 1)
                if n % 2 == 1:
                    filled(ins, key)

            for n in range(FT + 2):
                if n < FT:
                    sb_scores(n)
                if 1 <= n <= FT:
                    sb_sums(n - 1)
                if n >= 2:
                    sb_values(n - 2)
            transposed_o(1, [("so", n) for n in range(FT // 2)])
            by_tokens("wo1", AT["wo1"])

            transposed_h(3)
            b = begin(pe, "logits")
            for tb in range(TB):
                for t in range(DT):
                    ins = mm(b[:, tb * E:(tb + 1) * E], routed[:, t, tb * P:(tb + 1) * P], router[:, t, :], t == 0, t == DT - 1)
            filled(ins, "logits")
            pe.wait_ge(picks_ready, 1)
            chosen = route[:, 6, :, :]
            b = begin(pe, "places")
            mm(b[:, 0:E], before, chosen[:, 0, :], True, True)
            mm(b[:, E:2 * E], before, chosen[:, 1, :], True, False)
            mm(b[:, E:2 * E], ones[:, :], chosen[:, 0, :], False, True)
            mm(b[:, 2 * E:3 * E], ones[:, :], chosen[:, 0, :], True, False)
            filled(mm(b[:, 2 * E:3 * E], ones[:, :], chosen[:, 1, :], False, True), "places")

            def gather(name, i=None):
                for q in range(2):
                    b = begin(pe, (name, q), i)
                    for n in range(4):
                        for tb in range(TB):
                            t = 4 * q + n
                            ins = mm(b[:, n * CAP:(n + 1) * CAP], h[:, tb, t * P:(t + 1) * P], place[:, tb, :],
                                     tb == 0, tb == TB - 1)
                    filled(ins, (name, q))

            def gate_or_up(kind, b, i):
                n0, key = AT[("moe", kind, b)], (kind[0], b)
                out = begin(pe, key, i)
                for k in range(2):
                    w = unit(n0 + k, i)
                    for t in range(HALF_T):
                        tt = HALF_T * k + t
                        ins = product(out[0:CAP, :], (gathered_high[:, tt, :], gathered_low[:, tt, :]),
                                      (w[0][:, t, :], w[1][:, t, :]), tt == 0, tt == DT - 1)
                    if k == 0:
                        used_up(ins, n0)
                filled(ins, key)

            def transposed_hidden(b, i):
                taken(pe, ("u", b), i)
                out = begin(pe, ("hidT", b), i)
                for s in range(BT):
                    ins = nc.tensor.transpose(out[:, s * CAP:(s + 1) * CAP], e_prod[b % 2][:, s * P:(s + 1) * P],
                                              ident[0:CAP, 0:CAP])
                filled(ins, ("hidT", b))

            def expert_down(b, i):
                n0 = AT[("moe", "down", b)]
                taken(pe, ("hidT", b), i)
                for k in range(2):
                    w = unit(n0 + k, i)
                    wh, wl = by_rows(w[0]), by_rows(w[1])
                    for s in range(2):
                        c = (2 * k + s) * CAP
                        for dh in range(DH):
                            key = ("y", dh)
                            first = b == 0 and k == 0 and s == 0
                            last = b == BLOCKS - 1 and k == 1 and s == 1
                            out = begin(pe, key, i) if first else bank[:, USES[key][0], :]
                            cols = slice(dh * HALF, (dh + 1) * HALF)
                            ins = product(out[0:CAP, :], (hid_high[:, c:c + CAP], hid_low[:, c:c + CAP]),
                                          (wh[:, s, cols], wl[:, s, cols]), first, last)
                            if last:
                                filled(ins, key)
                    used_up(ins, n0 + k)

            def item(i, last):
                pe.wait_ge(gathered_ready, i * 2 + 2)
                for kind, b in block_order(BLOCKS):
                    if kind != "down":
                        gate_or_up(kind, b, i)
                    elif b < BLOCKS - 1:
                        expert_down(b, i)
                    if kind == "gate" and b >= 1:
                        transposed_hidden(b - 1, i)
                    elif kind == "up" and b == 0:
                        pe.wait_ge(weighted_ready, i + 1)
                        out = begin(pe, "gates", i)
                        for tb in range(TB):
                            ins = nc.tensor.transpose(out[0:CAP, tb * P:(tb + 1) * P], weighted[:, tb, :], ident)
                        filled(ins, "gates")
                    elif kind == "down" and b == BLOCKS - 2:
                        transposed_hidden(BLOCKS - 1, i)
                        if not last:
                            pe.wait_ge(place_ready, i + 2)
                            gather("gather", i)
                expert_down(BLOCKS - 1, i)
                if not last:
                    pe.wait_ge(gathered_ready, i * 2 + 4)
                taken(pe, "gates", i)
                for dh in range(DH):
                    taken(pe, ("y", dh), i)
                for n in range(TB * DH):
                    tb, dh = n // DH, n % DH
                    out = begin(pe, ("scatter", n), i)
                    filled(mm(out, gates[:, tb * P:(tb + 1) * P], y_sb[:, dh * HALF:(dh + 1) * HALF], True, True),
                           ("scatter", n))

            pe.wait_ge(place_ready, 1)
            gather("first gather")
            pe.wait_ge(items_ready, 1)
            items = pe.value_load(n_items[0:1, 0:1], min_val=E, max_val=PASSES * E)
            with pe.Fori(0, items - 1) as i:
                item(i, False)
            item(items - 1, True)


INPUTS = ["x", "rel_bias", "attn_norm", "ffn_norm", "final_norm", "swa_w_qkv", "swa_b_qkv", "swa_sinks", "swa_w_o",
          "sb_w_qkv", "sb_w_o", "ffn_w_gate", "ffn_w_up", "ffn_w_down", "moe_router", "moe_w_gate", "moe_w_up",
          "moe_w_down"]


def kernel(**inputs):
    import concourse.bacc as bacc
    from concourse.bass_utils import run_bass_kernel_spmd

    nc = bacc.Bacc("TRN2", target_bir_lowering=False, num_devices=1)
    arrays = {name: np.ascontiguousarray(inputs[name]) for name in INPUTS}
    arrays["consts"] = constants()
    arrays["onehot"] = bucket_rows()
    a = {name: nc.dram_tensor(f"in_{name}", v.shape, F32, kind="ExternalInput").ap() for name, v in arrays.items()}
    a["out"] = nc.dram_tensor("result", (1, SEQ, D), F32, kind="ExternalOutput").ap()
    build(nc, a)
    result = run_bass_kernel_spmd(nc, [{f"in_{name}": v for name, v in arrays.items()}], core_ids=[0])
    return result.results[0]["result"]
```
